# Optimizing a Trainium2 kernel written in Bass

```python
import jax, jax.numpy as jnp
from jax import lax
import numpy as np

D_MODEL = 1024
BATCH = 1
SEQ = 4096
DEPTH = 1

D_MIX = D_MODEL
POOL_WIDTH = D_MIX // 2
RWKV_WIDTH = D_MIX - POOL_WIDTH
POOL_WINDOWS = (2, 4, 8, 16)
POOL_GROUPS = len(POOL_WINDOWS)
POOL_GROUP_DIM = POOL_WIDTH // POOL_GROUPS
RWKV_HEAD_DIM = 64
RWKV_HEADS = RWKV_WIDTH // RWKV_HEAD_DIM
DECAY_LORA = 64
ICLR_LORA = 64
GN_EPS = 64e-5
NORM_EPS = 1e-6

OFF_POOL_V = 0
OFF_POOL_G = OFF_POOL_V + POOL_WIDTH
OFF_R = OFF_POOL_G + POOL_WIDTH
OFF_K = OFF_R + RWKV_WIDTH
OFF_V = OFF_K + RWKV_WIDTH
OFF_WD = OFF_V + RWKV_WIDTH
OFF_AD = OFF_WD + DECAY_LORA
OFF_RG = OFF_AD + ICLR_LORA
D_IN_PROJ = OFF_RG + RWKV_WIDTH
SHIFT_COLS = OFF_RG - OFF_R

kernel_name = "hymba_pool_rwkv7_hybrid"

def rms_norm(x, gain):
    xf = x.astype(jnp.float32)
    y = xf * lax.rsqrt(jnp.mean(xf * xf, axis=-1, keepdims=True) + NORM_EPS)
    return (y * gain.astype(jnp.float32)).astype(x.dtype)

def token_shift(u):
    return jnp.pad(u, ((0, 0), (1, 0), (0, 0)))[:, :-1]

def multiscale_pool(u, pool_w, pool_scale):
    b, s, _ = u.shape
    uf = u.astype(jnp.float32)
    cs = jnp.pad(jnp.cumsum(uf, axis=1), ((0, 0), (1, 0), (0, 0)))
    t = jnp.arange(s)
    diffs = []
    for g, win in enumerate(POOL_WINDOWS):
        sl = slice(g * POOL_GROUP_DIM, (g + 1) * POOL_GROUP_DIM)
        hi = cs[:, 1:, sl]
        lo = jnp.pad(cs[:, :s + 1 - win, sl], ((0, 0), (win - 1, 0), (0, 0)))
        cnt = jnp.minimum(t + 1, win).astype(jnp.float32)[None, :, None]
        diffs.append((hi - lo) / cnt - uf[..., sl])
    d = jnp.stack(diffs, axis=2)
    y = jnp.einsum('bsgi,gio->bsgo', d, pool_w.astype(jnp.float32))
    return y.reshape(b, s, POOL_WIDTH) * pool_scale.astype(jnp.float32)

def wkv7_scan(r, decay, k, v, a_vec, b_vec):
    bsz, _, h, n = r.shape
    xs = tuple(jnp.swapaxes(z, 0, 1) for z in (r, decay, k, v, a_vec, b_vec))

    def step(state, inp):
        r_t, w_t, k_t, v_t, a_t, b_t = inp
        sa = jnp.einsum('bhij,bhj->bhi', state, a_t)
        state = (state * w_t[:, :, None, :]
                 + sa[..., :, None] * b_t[..., None, :]
                 + v_t[..., :, None] * k_t[..., None, :])
        y = jnp.einsum('bhij,bhj->bhi', state, r_t)
        return state, y

    s0 = jnp.zeros((bsz, h, n, n), jnp.float32)
    _, ys = lax.scan(step, s0, xs)
    return jnp.swapaxes(ys, 0, 1)

def rwkv7_branch(p, mu, w0, w_lora_up, a0, a_lora_up, k_k, k_a, r_k, lnx_w, lnx_b):
    b, s, _ = p.shape
    pf = p.astype(jnp.float32)
    pf = pf + (token_shift(pf) - pf) * mu.astype(jnp.float32)
    r = pf[..., 0:RWKV_WIDTH]
    k = pf[..., RWKV_WIDTH:2 * RWKV_WIDTH]
    v = pf[..., 2 * RWKV_WIDTH:3 * RWKV_WIDTH]
    wd = pf[..., 3 * RWKV_WIDTH:3 * RWKV_WIDTH + DECAY_LORA]
    ad = pf[..., 3 * RWKV_WIDTH + DECAY_LORA:]
    w_log = -jax.nn.softplus(-(w0 + jnp.tanh(wd) @ w_lora_up.astype(jnp.float32))) - 0.5
    decay = jnp.exp(-jnp.exp(w_log))
    a = jax.nn.sigmoid(a0 + ad @ a_lora_up.astype(jnp.float32))
    hs = (b, s, RWKV_HEADS, RWKV_HEAD_DIM)
    kk = (k * k_k).reshape(hs)
    kk = kk * lax.rsqrt(jnp.sum(kk * kk, axis=-1, keepdims=True) + 1e-12)
    k = k * (1.0 + (a - 1.0) * k_a)
    r_h, k_h, v_h, a_h = r.reshape(hs), k.reshape(hs), v.reshape(hs), a.reshape(hs)
    y = wkv7_scan(r_h, decay.reshape(hs), k_h, v_h, -kk, kk * a_h)
    mean = jnp.mean(y, axis=-1, keepdims=True)
    var = jnp.mean(jnp.square(y - mean), axis=-1, keepdims=True)
    y = ((y - mean) * lax.rsqrt(var + GN_EPS)).reshape(b, s, RWKV_WIDTH)
    y = y * lnx_w + lnx_b
    bonus = jnp.sum(r_h * k_h * r_k, axis=-1, keepdims=True) * v_h
    return y + bonus.reshape(b, s, RWKV_WIDTH)

def setup_inputs(seed: int = 0) -> dict:
    key = jax.random.key(seed)
    ks = jax.random.split(key, 24)
    f = jnp.float32
    L = DEPTH
    nrm = lambda k, shp, sc: jax.random.normal(k, shp, f) * sc
    return {
        "x": jax.random.normal(ks[0], (BATCH, SEQ, D_MODEL), f),
        "c": jax.random.normal(ks[1], (BATCH, D_MODEL), f),
        "w_ada": nrm(ks[2], (L, D_MODEL, 3 * D_MODEL), D_MODEL ** -0.5),
        "b_ada": nrm(ks[3], (L, 3 * D_MODEL), 0.01),
        "norm_gain": 1.0 + nrm(ks[4], (L, D_MODEL), 0.05),
        "w_in": nrm(ks[5], (L, D_MODEL, D_IN_PROJ), D_MODEL ** -0.5),
        "pool_w": nrm(ks[6], (L, POOL_GROUPS, POOL_GROUP_DIM, POOL_GROUP_DIM), POOL_GROUP_DIM ** -0.5),
        "pool_scale": 1.0 + nrm(ks[7], (L, POOL_WIDTH), 0.1),
        "mu": jax.random.uniform(ks[8], (L, SHIFT_COLS), f),
        "w0": jax.random.uniform(ks[9], (L, RWKV_WIDTH), f, minval=-6.0, maxval=1.0),
        "w_lora_up": nrm(ks[10], (L, DECAY_LORA, RWKV_WIDTH), 0.1 * DECAY_LORA ** -0.5),
        "a0": nrm(ks[11], (L, RWKV_WIDTH), 0.1),
        "a_lora_up": nrm(ks[12], (L, ICLR_LORA, RWKV_WIDTH), 0.1 * ICLR_LORA ** -0.5),
        "k_k": 0.85 + nrm(ks[13], (L, RWKV_WIDTH), 0.05),
        "k_a": 1.0 + nrm(ks[14], (L, RWKV_WIDTH), 0.05),
        "r_k": nrm(ks[15], (L, RWKV_HEADS, RWKV_HEAD_DIM), 0.1),
        "lnx_w": 1.0 + nrm(ks[16], (L, RWKV_WIDTH), 0.05),
        "lnx_b": nrm(ks[17], (L, RWKV_WIDTH), 0.01),
        "w_out": nrm(ks[18], (L, D_MIX, D_MODEL), D_MIX ** -0.5),
        "final_gain": 1.0 + nrm(ks[19], (D_MODEL,), 0.05),
    }

def reference(x, c, w_ada, b_ada, norm_gain, w_in, pool_w, pool_scale, mu, w0, w_lora_up,
              a0, a_lora_up, k_k, k_a, r_k, lnx_w, lnx_b, w_out, final_gain):
    h = x
    for l in range(DEPTH):
        mod = jax.nn.silu(c) @ w_ada[l] + b_ada[l]
        shift, scale, gate = jnp.split(mod, 3, axis=-1)
        u = rms_norm(h, norm_gain[l]) * (1.0 + scale[:, None, :]) + shift[:, None, :]
        proj = u @ w_in[l]
        y_pool = multiscale_pool(proj[..., OFF_POOL_V:OFF_POOL_G], pool_w[l], pool_scale[l])
        y_pool = y_pool * jax.nn.silu(proj[..., OFF_POOL_G:OFF_R].astype(jnp.float32))
        y_rwkv = rwkv7_branch(proj[..., OFF_R:OFF_RG], mu[l], w0[l], w_lora_up[l], a0[l],
                              a_lora_up[l], k_k[l], k_a[l], r_k[l], lnx_w[l], lnx_b[l])
        y_rwkv = y_rwkv * jax.nn.silu(proj[..., OFF_RG:].astype(jnp.float32))
        y = jnp.concatenate([y_pool, y_rwkv], axis=-1).astype(h.dtype) @ w_out[l]
        h = h + gate[:, None, :] * y
    return rms_norm(h, final_gain)


_drawn_inputs = setup_inputs


def setup_inputs(seed=0):
    import zlib

    import numpy as np

    out = dict(_drawn_inputs(seed))
    spreads = {}
    factors = {'b_ada': 4.5, 'w_lora_up': 8.0, 'a0': 3.273, 'lnx_w': 3.616, 'lnx_b': 27.007}
    for name, (base, spread) in spreads.items():
        noise = np.random.default_rng([zlib.crc32(name.encode()), seed]).standard_normal(out[name].shape)
        drawn = base * np.exp(spread * noise) if base else spread * noise
        out[name] = __import__('jax').numpy.asarray(drawn.astype(out[name].dtype))
    for name, factor in factors.items():
        out[name] = (out[name] * factor).astype(out[name].dtype)
    return out
```

```python
from contextlib import ExitStack
import math

import concourse.bass as bass
from concourse import mybir

F32 = mybir.dt.float32
BF16 = mybir.dt.bfloat16
ALU = mybir.AluOpType
ACT = mybir.ActivationFunctionType
AX = mybir.AxisListType

P = 128
D = 1024
KT = D // P
SEQ = 4096
POOLW = 512
PT = POOLW // P
RW = 512
NP = RW // P
HD = 64
LORA = 64
WIN = (2, 4, 8, 16)
HALO = 15
EPS = 1e-6
GN_EPS = 64e-5
KK_EPS = 1e-12
DECAY = math.exp(-0.5)

T1 = 256
N1 = SEQ // T1
T2 = 128
N2 = SEQ // T2
C = 64
NC = T2 // C
MIX = 13
POOL_COLS = 2 * POOLW
R_COLS = MIX * P + RW
RT = R_COLS // P
INV = 14
ACT_OWN = 4
DVE_OWN = 36
LN_MAX = 1e19

ROWS = {}
for _n, _k in (("b_ada", 24), ("norm_gain", 8), ("mu", 13), ("pool_scale", 4), ("w0", 4), ("a0", 4),
               ("k_k", 4), ("k_a", 4), ("r_k", 4), ("lnx_w", 4), ("lnx_b", 4), ("c", 8)):
    ROWS[_n] = (sum(k for _, k in ROWS.values()), _k)
NROWS = sum(k for _, k in ROWS.values())


class Signal:

    def __init__(self, sem, per, start=0):
        self.sem, self.per, self.start = sem, per, start

    def at(self, n, k):
        return n * self.per + (self.start + k)


class Steps:

    def __init__(self, eng, own):
        self.eng, self.own = eng, own

    def block(self, n):
        self.n, self.count = n, {}

    def __call__(self, ins, signal=None, hold=True):
        s = signal or self.own
        self.count[s] = self.count.get(s, 0) + 1
        ins.then_inc(s.sem, 1)
        if hold:
            self.eng.wait_ge(s.sem, s.at(self.n, self.count[s]))

    def wait(self, signal, k, back=0):
        self.eng.wait_ge(signal.sem, signal.at(self.n, k - back * signal.per))

    def end(self, name, full=True):
        for s, k in self.count.items():
            if full:
                assert k == s.per, (name, s.sem.name, k, s.per)


def rows_of(view, n):
    if isinstance(n, int):
        return view[n]
    part = view[bass.ds(n, 1)]
    return part.rearrange("a p d -> (a p) d") if len(part.shape) == 3 else part.rearrange("a p j d -> (a p) j d")


def let_through(sp, gate):
    sp.sem_inc(gate, 1)


def wide(v):
    return v.unsqueeze(2).broadcast_to([P, NP, T2])


def chunks(t):
    return t.rearrange("p a (c t) -> p a c t", t=C)


def half(e):
    return slice(HD * e, HD * e + HD)


def build(nc, A, out):
    h1 = nc.dram_tensor("h1_dram", (SEQ, D), F32, kind="Internal").ap()
    ctx = ExitStack()
    with ctx:
        def sb(name, shape, dt=F32, stack=ctx):
            return stack.enter_context(nc.sbuf_tensor(name, shape, dt))

        def sem(name, stack=ctx):
            return stack.enter_context(nc.semaphore(name))

        bank = [ctx.enter_context(nc.psum_tensor(f"bank{b}", [P, 512], F32)) for b in range(8)]

        w2 = sb("w2", [P, KT, R_COLS])
        wo2 = sb("wo2", [P, NP, D])
        up = sb("up", [P, RW])
        ident = sb("ident", [P, P])
        center = sb("center", [P, P])
        head_mean = sb("head_mean", [P, P])
        head_sum = sb("head_sum", [P, P])
        rk_sum = sb("rk_sum", [P, NP, P])
        gram_mask = sb("gram_mask", [P, P])
        diag16 = sb("diag16", [P, HD])
        off16 = sb("off16", [P, HD])
        ident64 = sb("ident64", [P, HD])
        ones = sb("ones", [P, HD])
        restart = sb("restart", [P, NP * T2])
        fgain = sb("fgain", [P, D])
        gate_row = sb("gate_row", [P, D])
        rows = sb("rows", [P, P])
        vec = sb("vec", [P, NROWS])
        mod = sb("mod", [P, 16])
        gsc = sb("gsc", [P, KT])
        sc = sb("sc", [P, 3, KT])
        b1 = sb("b1", [P, 2 * PT])
        nb1 = sb("nb1", [P, PT])
        b2 = sb("b2", [P, RT])
        omu = sb("omu", [P, MIX])
        omub = sb("omub", [P, MIX])
        mub = sb("mub", [P, MIX])
        negv = sb("negv", [P, 2, NP])
        oka = sb("oka", [P, NP])
        eps = sb("eps", [P, 3])

        def v(name, t=0, n=1):
            return vec[:, ROWS[name][0] + t:ROWS[name][0] + t + n]

        pass1 = ExitStack()
        w1 = sb("w1", [P, KT, POOL_COLS], stack=pass1)
        wo1 = sb("wo1", [P, PT, D], stack=pass1)
        poolw = sb("poolw", [P, PT, P], stack=pass1)

        w2_loaded = sem("w2_loaded")
        sp_gate = sem("sp_gate")
        w_in_v = A["w_in"][0].rearrange("(k p) n -> p k n", p=P)
        w_out_v = A["w_out"][0].rearrange("(k p) n -> p k n", p=P)

        with ExitStack() as st:
            stage = sb("stage", [P, 3, KT, P], stack=st)
            bgate = sb("bgate", [P, D], stack=st)
            rows_in, w_in1, small_in = sem("rows_in", st), sem("w_in1", st), sem("small_in", st)
            staged = [sem(f"staged{j}", st) for j in range(3)]
            used = sem("stage_used", st)
            consts, vec_ps, vec_ok = sem("consts", st), sem("vec_ps", st), sem("vec_ok", st)
            sc_exp, sc_ok, mod_ps = sem("sc_exp", st), sem("sc_ok", st), sem("mod_ps", st)
            mod_ok, b1_ps, dve_link, pool_link = (sem("mod_ok", st), sem("b1_ps", st), sem("dve_link", st),
                                                  sem("pool_link", st))
            ada = A["w_ada"][0].rearrange("(k p) n -> p k n", p=P)
            flat = {"r_k": A["r_k"][0].rearrange("h d -> (h d)"), "c": A["c"][0]}

            with nc.Block() as block:
                @block.sync
                def _(sp):
                    for name, (r0, k) in ROWS.items():
                        src = flat[name] if name in flat else A[name][0]
                        sp.dma_start(rows[r0:r0 + k, :], src.rearrange("(k p) -> k p", p=P)).then_inc(rows_in, 16)
                    for j in range(24):
                        if j >= 3:
                            sp.wait_ge(used, j - 2)
                        sp.dma_start(stage[:, j % 3], ada[:, :, j * P:(j + 1) * P]).then_inc(staged[j % 3], 16)

                @block.scalar
                def _(act):
                    act.dma_start(bgate[:, :], A["b_ada"][:, 2 * D:3 * D].partition_broadcast(P)).then_inc(small_in, 16)
                    act.dma_start(fgain[:, :], A["final_gain"].rearrange("(a n) -> a n", a=1).partition_broadcast(P)).then_inc(small_in, 16)
                    act.dma_start(poolw[:, :, :], A["pool_w"][0].rearrange("g i o -> i g o")).then_inc(small_in, 16)
                    act.dma_start(up[0:LORA, :], A["w_lora_up"][0]).then_inc(small_in, 16)
                    act.dma_start(up[LORA:P, :], A["a_lora_up"][0]).then_inc(small_in, 16)
                    act.dma_start(w1[:, :, :], w_in_v[:, :, 0:POOL_COLS]).then_inc(w_in1, 16)
                    act.dma_start(wo1[:, :, :], w_out_v[:, 0:PT, :]).then_inc(w_in1, 16)
                    nc.scalar.preload_act_table_set("natural_log_exp_and_others")
                    act.wait_ge(vec_ok, 1)
                    nc.scalar.activation(sc[:, 0, :], v("c", 0, 8), ACT.Exp, scale=-1.0).then_inc(sc_exp, 1)

                @block.gpsimd
                def _(pool):
                    n = [0]

                    def link(ins):
                        n[0] += 1
                        ins.then_inc(pool_link, 1)
                        pool.wait_ge(pool_link, n[0])

                    def band(t, pattern, base, mult, op, fill):
                        link(nc.gpsimd.affine_select(out=t, in_=t, compare_op=op, fill=fill, base=base,
                                                     pattern=pattern, channel_multiplier=mult))

                    link(nc.gpsimd.memset(ident[:, :], 0.0))
                    band(ident[:, :], [[-1, P]], 0, 1, ALU.not_equal, 1.0)
                    link(nc.gpsimd.memset(ones[:, :], 1.0))
                    link(nc.gpsimd.memset(ident64[:, :], 0.0))
                    band(ident64[:, :], [[-1, HD]], 0, 1, ALU.not_equal, 1.0)
                    band(ident64[:, :], [[-1, HD]], -HD, 1, ALU.not_equal, 1.0)
                    link(nc.gpsimd.memset(head_sum[:, :], 0.0))
                    link(nc.gpsimd.memset(head_sum[0:HD, 0:HD], 1.0))
                    link(nc.gpsimd.memset(head_sum[HD:P, HD:P], 1.0))
                    link(nc.gpsimd.tensor_scalar(head_mean[:, :], head_sum[:, :], 1.0 / HD, None, ALU.mult))
                    link(nc.gpsimd.tensor_tensor(center[:, :], ident[:, :], head_mean[:, :], ALU.subtract))
                    link(nc.gpsimd.memset(gram_mask[:, :], 1.0))
                    for e in range(2):
                        g = gram_mask[half(e), :]
                        band(g[:, 0:HD], [[1, HD]], 0, -1, ALU.is_gt, 0.0)
                        band(g[:, HD:P], [[1, HD]], 0, -1, ALU.is_ge, 0.0)
                    link(nc.gpsimd.memset(diag16[:, :], 1.0))
                    for e in range(2):
                        d = diag16[half(e), :].rearrange("p (b j) -> p b j", j=16)
                        band(d, [[-16, 4], [0, 16]], 0, 1, ALU.is_ge, 0.0)
                        band(d, [[16, 4], [0, 16]], 15, -1, ALU.is_ge, 0.0)
                    link(nc.gpsimd.tensor_scalar(off16[:, :], diag16[:, :], -1.0, 1.0, ALU.mult, ALU.add))
                    link(nc.gpsimd.memset(restart[:, :], 1.0))
                    link(nc.gpsimd.memset(restart[:, :].rearrange("p (c t) -> p c t", t=C)[:, :, 0:1], 0.0))
                    for j, e in enumerate((EPS, KK_EPS, GN_EPS)):
                        link(nc.gpsimd.memset(eps[:, j:j + 1], e))
                    nc.gpsimd.memset(eps[:, 0:1], EPS).then_inc(consts, 1)

                @block.tensor
                def _(pe):
                    pe.wait_ge(rows_in, 16 * len(ROWS))
                    pe.wait_ge(consts, 1)
                    nc.tensor.transpose(bank[0][:, 0:NROWS], rows[0:NROWS, :], ident[0:NROWS, 0:NROWS]).then_inc(vec_ps, 1)
                    pe.wait_ge(sc_ok, 1)
                    for j in range(24):
                        pe.wait_ge(staged[j % 3], 16 * (j // 3 + 1))
                        for k in range(KT):
                            col = sc[:, 2, k:k + 1]
                            if j < 16:
                                last = nc.tensor.matmul(bank[1][:, j:j + 1], stage[:, j % 3, k], col,
                                                        start=(k == 0), stop=(k == KT - 1))
                            else:
                                g = j - 16
                                last = nc.tensor.matmul(bank[2 + g // 4][:, (g % 4) * P:(g % 4 + 1) * P],
                                                        col.broadcast_to([P, P]), stage[:, j % 3, k],
                                                        start=(k == 0), stop=(k == KT - 1))
                        last.then_inc(used, 1)
                    pe.wait_ge(mod_ok, 1)
                    pe.wait_ge(w_in1, 32)
                    for t in range(2 * PT):
                        for k in range(KT):
                            last = nc.tensor.matmul(bank[4][:, t:t + 1], w1[:, k, t * P:(t + 1) * P], mod[:, k:k + 1],
                                                    start=(k == 0), stop=(k == KT - 1))
                    last.then_inc(b1_ps, 1)

                @block.vector
                def _(dve):
                    n = [0]

                    def link(ins):
                        n[0] += 1
                        ins.then_inc(dve_link, 1)
                        dve.wait_ge(dve_link, n[0])

                    dve.wait_ge(vec_ps, 1)
                    nc.vector.tensor_copy(vec[:, :], bank[0][:, 0:NROWS]).then_inc(vec_ok, 1)
                    dve.wait_ge(vec_ok, 1)
                    dve.wait_ge(consts, 1)
                    dve.wait_ge(sc_exp, 1)
                    link(nc.vector.tensor_scalar_add(sc[:, 0, :], sc[:, 0, :], 1.0))
                    link(nc.vector.reciprocal(sc[:, 1, :], sc[:, 0, :]))
                    nc.vector.tensor_tensor(sc[:, 2, :], sc[:, 1, :], v("c", 0, 8), ALU.mult).then_inc(sc_ok, 1)
                    link(nc.vector.tensor_scalar(omu[:, :], v("mu", 0, MIX), -1.0, 1.0, ALU.mult, ALU.add))
                    link(nc.vector.tensor_scalar(negv[:, 0, :], v("w0", 0, NP), -1.0, None, ALU.mult))
                    link(nc.vector.tensor_scalar(negv[:, 1, :], v("a0", 0, NP), -1.0, None, ALU.mult))
                    link(nc.vector.tensor_scalar(oka[:, :], v("k_a", 0, NP), -1.0, 1.0, ALU.mult, ALU.add))
                    for p in range(NP):
                        link(nc.vector.tensor_scalar(rk_sum[:, p], head_sum[:, :], v("r_k", p), None, ALU.mult))
                    dve.wait_ge(used, 16)
                    nc.vector.tensor_tensor(mod[:, :], bank[1][:, 0:16], v("b_ada", 0, 16), ALU.add).then_inc(mod_ok, 1)
                    dve.wait_ge(mod_ok, 1)
                    link(nc.vector.tensor_scalar_add(gsc[:, :], mod[:, 8:16], 1.0))
                    link(nc.vector.tensor_tensor(gsc[:, :], gsc[:, :], v("norm_gain", 0, KT), ALU.mult))
                    dve.wait_ge(used, 24)
                    dve.wait_ge(small_in, 80)
                    for h in range(2):
                        link(nc.vector.tensor_tensor(gate_row[:, h * 512:(h + 1) * 512], bank[2 + h][:, :],
                                                     bgate[:, h * 512:(h + 1) * 512], ALU.add))
                    dve.wait_ge(w_in1, 32)
                    for k in range(PT):
                        link(nc.vector.scalar_tensor_tensor(out=wo1[:, k, :], in0=wo1[:, k, :], scalar=v("pool_scale", k),
                                                            in1=gate_row[:, :], op0=ALU.mult, op1=ALU.mult))
                    dve.wait_ge(b1_ps, 1)
                    link(nc.vector.tensor_copy(b1[:, :], bank[4][:, 0:2 * PT]))
                    link(nc.vector.tensor_scalar(nb1[:, :], b1[:, PT:2 * PT], -1.0, None, ALU.mult))
                    for k in range(KT):
                        link(nc.vector.tensor_scalar(w1[:, k, :], w1[:, k, :], gsc[:, k:k + 1], None, ALU.mult))

        with pass1 as st:
            x_in = sb("x_in", [P, 2, D], stack=st)
            xr = sb("xr", [P, 2, D], stack=st)
            junk = sb("junk", [P, D], BF16, stack=st)
            stat = sb("stat", [P, 3, 2], stack=st)
            xT = sb("xT", [P, KT, T1], stack=st)
            u = sb("u", [P, PT, HALO + T1], stack=st)
            gate = sb("gate", [P, PT, T1], stack=st)
            win_a = sb("win_a", [P, PT, HALO + T1], stack=st)
            win_b = sb("win_b", [P, PT, HALO + T1], stack=st)
            diff = sb("diff", [P, PT, T1], stack=st)
            yc = sb("yc", [P, PT, T1], stack=st)
            inv_cnt = sb("inv_cnt", [P, PT, 16], stack=st)

            x_loaded = sem("x_loaded", st)
            xr_loaded = [sem(f"xr_loaded{j}", st) for j in range(2)]
            h_stored = [sem(f"h_stored{j}", st) for j in range(2)]
            cnt_ready = sem("cnt_ready", st)
            norm_own = Signal(sem("norm_own", st), 5)
            halo_ready = Signal(sem("halo_ready", st), 1)
            gate_own = Signal(sem("gate_own", st), 2)
            diff_first = Signal(sem("diff_first", st), 2 * PT)
            win_own = Signal(sem("win_own", st), 0)
            xn_ready = Signal(sem("xn_ready", st), 1)
            xT_ps = Signal(sem("xT_ps", st), 4)
            xT_ready = Signal(sem("xT_ready", st), 4)
            proj_ps = Signal(sem("proj_ps", st), 4)
            u_ready = Signal(sem("u_ready", st), PT)
            gx_ready = Signal(sem("gx_ready", st), PT)
            gate_ready = Signal(sem("gate_ready", st), PT)
            win_ready = Signal(sem("win_ready", st), PT)
            diff_ready = Signal(sem("diff_ready", st), PT)
            pool_ps = Signal(sem("pool_ps", st), 2)
            yc_ready = Signal(sem("yc_ready", st), 2)
            out_ps = Signal(sem("out_ps", st), 4)
            h_ready = Signal(sem("h_ready", st), 4)

            x_v = A["x"][0].rearrange("(n j p) d -> n p j d", p=P, j=2)
            x_t = A["x"][0].rearrange("(m p) d -> m p d", p=P)
            h1_t = h1.rearrange("(m p) d -> m p d", p=P)
            win = [win_a, win_b, win_a, win_b]

            with nc.Block() as block:
                @block.sync
                def _(sp):
                    def load_x(n):
                        let_through(sp, sp_gate)
                        sp.dma_start(x_in[:, :, :], rows_of(x_v, n)).then_inc(x_loaded, 16)

                    def load_residual(n):
                        let_through(sp, sp_gate)
                        for j in range(2):
                            sp.dma_start(xr[:, j], rows_of(x_t, 2 * n + j)).then_inc(xr_loaded[j], 16)

                    def store(n):
                        for j in range(2):
                            sp.wait_ge(h_ready.sem, h_ready.at(n, 2 * j + 2))
                            let_through(sp, sp_gate)
                            sp.dma_start(rows_of(h1_t, 2 * n + j), xr[:, j]).then_inc(h_stored[j], 16)

                    def step(n, more):
                        if more:
                            sp.wait_ge(xT_ps.sem, xT_ps.at(n, 4))
                            load_x(n + 1)
                        store(n - 1)
                        for j in range(2):
                            sp.wait_ge(h_stored[j], n * 16)
                        load_residual(n)

                    load_x(0)
                    load_residual(0)
                    sp.wait_ge(xT_ps.sem, xT_ps.at(0, 4))
                    load_x(1)
                    with sp.Fori(1, N1 - 1) as n:
                        step(n, True)
                    step(N1 - 1, False)
                    store(N1 - 1)
                    for j in range(2):
                        sp.wait_ge(h_stored[j], 16 * N1)

                @block.tensor
                def _(pe):
                    s = Steps(pe, None)

                    def transposes(n, first=False):
                        s.block(n)
                        s.wait(xn_ready, 1)
                        if not first:
                            s.wait(gx_ready, PT, back=1)
                            s.wait(gate_ready, PT, back=1)
                        for b in range(4):
                            for q in range(4):
                                k, j = 2 * b + q // 2, q % 2
                                last = nc.tensor.transpose(bank[b][:, q * P:(q + 1) * P], x_in[:, j, k * P:(k + 1) * P], ident[:, :])
                            last.then_inc(xT_ps.sem, 1)

                    def project(n):
                        s.block(n)
                        s.wait(xT_ready, 4)
                        for t in range(2 * PT):
                            for k in range(KT):
                                last = nc.tensor.matmul(bank[t // 2][:, (t % 2) * T1:(t % 2 + 1) * T1], w1[:, k, t * P:(t + 1) * P],
                                                        xT[:, k, :], start=(k == 0), stop=(k == KT - 1))
                            if t % 2:
                                last.then_inc(proj_ps.sem, 1)

                    def finish(n, first=False):
                        s.block(n)
                        s.wait(diff_ready, PT)
                        if not first:
                            s.wait(yc_ready, 2, back=1)
                        for g in range(PT):
                            last = nc.tensor.matmul(bank[4 + g // 2][:, (g % 2) * T1:(g % 2 + 1) * T1], poolw[:, g, :],
                                                    diff[:, g, :], start=True, stop=True)
                            if g % 2:
                                last.then_inc(pool_ps.sem, 1)
                        s.wait(yc_ready, 2)
                        for j in range(2):
                            for h in range(2):
                                if j:
                                    s.wait(h_ready, h + 1)
                                elif not first:
                                    s.wait(h_ready, 3 + h, back=1)
                                for k in range(PT):
                                    last = nc.tensor.matmul(bank[6 + h][:, :], yc[:, k, j * P:(j + 1) * P],
                                                            wo1[:, k, h * 512:(h + 1) * 512], start=(k == 0), stop=(k == PT - 1))
                                last.then_inc(out_ps.sem, 1)

                    transposes(0, first=True)
                    project(0)
                    transposes(1)
                    project(1)
                    finish(0, first=True)
                    transposes(2)
                    with pe.Fori(2, N1 - 1) as n:
                        project(n)
                        finish(n - 1)
                        transposes(n + 1)
                    project(N1 - 1)
                    finish(N1 - 2)
                    finish(N1 - 1)

                @block.scalar
                def _(act):
                    s = Steps(act, norm_own)
                    nc.scalar.preload_act_table_set("natural_log_exp_and_others")

                    def norm(n, first=False):
                        s.block(n)
                        act.wait_ge(x_loaded, n * 16 + 16)
                        for j in range(2):
                            s(nc.scalar.activation(junk[:, :], x_in[:, j, :], ACT.Square, accum_out=stat[:, 0, j:j + 1]))
                        s(nc.scalar.activation(stat[:, 1, :], stat[:, 0, :], ACT.Ln, scale=1.0 / D, bias=eps[:, 0:1]))
                        s(nc.scalar.activation(stat[:, 2, :], stat[:, 1, :], ACT.Exp, scale=-0.5))
                        s(nc.scalar.activation(x_in[:, 0, :], x_in[:, 0, :], ACT.Copy, scale=stat[:, 2, 0:1]))
                        s(nc.scalar.activation(x_in[:, 1, :], x_in[:, 1, :], ACT.Copy, scale=stat[:, 2, 1:2]), xn_ready)
                        for b in range(4):
                            s.wait(xT_ps, b + 1)
                            s(nc.scalar.activation(xT[:, 2 * b:2 * b + 2, :].rearrange("p k t -> p (k t)"), bank[b][:, :],
                                                   ACT.Copy), xT_ready)

                    def evacuate(n, first=False):
                        s.block(n)
                        if first:
                            s(nc.scalar.activation(u[:, :, 0:HALO], ident[:, 0:PT * HALO].rearrange("p (g h) -> p g h", g=PT),
                                                   ACT.Copy, scale=0.0), halo_ready)
                        else:
                            s.wait(diff_ready, PT, back=1)
                            s(nc.scalar.activation(u[:, :, 0:HALO], u[:, :, T1:T1 + HALO], ACT.Copy), halo_ready)
                        for g in range(PT):
                            s.wait(proj_ps, g // 2 + 1)
                            s(nc.scalar.activation(u[:, g, HALO:], bank[g // 2][:, (g % 2) * T1:(g % 2 + 1) * T1], ACT.Identity,
                                                   bias=b1[:, g:g + 1]), u_ready)
                        if not first:
                            s.wait(yc_ready, 2, back=1)
                        for g in range(PT):
                            s.wait(proj_ps, g // 2 + 3)
                            s(nc.scalar.activation(gate[:, g, :], bank[2 + g // 2][:, (g % 2) * T1:(g % 2 + 1) * T1], ACT.Exp,
                                                   scale=-1.0, bias=nb1[:, g:g + 1]), gx_ready)

                    norm(0, first=True)
                    evacuate(0, first=True)
                    norm(1)
                    with act.Fori(1, N1 - 1) as n:
                        evacuate(n)
                        norm(n + 1)
                    evacuate(N1 - 1)

                @block.gpsimd
                def _(pool):
                    for k in range(KT):
                        pool.dma_start(w2[:, k], w_in_v[:, k, POOL_COLS:]).then_inc(w2_loaded, 16)
                    pool.dma_start(wo2[:, :, :], w_out_v[:, PT:, :]).then_inc(w2_loaded, 16)
                    s = Steps(pool, win_own)
                    for g, w in enumerate(WIN):
                        for t in range(16):
                            last = nc.gpsimd.memset(inv_cnt[:, g, t:t + 1], 1.0 / min(t + 1, w))
                    last.then_inc(cnt_ready, 1)

                    def windows(n, first=False):
                        s.block(n)
                        if not first:
                            s.wait(diff_ready, PT, back=1)
                        s.wait(u_ready, PT)
                        src = u
                        for g in range(PT):
                            w = WIN[g]
                            s(nc.gpsimd.tensor_tensor(win[g][:, g:, w - 1:], src[:, g:, w - 1:], src[:, g:, w - 1 - w // 2:HALO + T1 - w // 2],
                                                      ALU.add), win_ready)
                            src = win[g]

                    windows(0, first=True)
                    with pool.Fori(1, N1) as n:
                        windows(n)

                @block.vector
                def _(dve):
                    s = Steps(dve, gate_own)
                    dve.wait_ge(cnt_ready, 1)

                    def gates(n):
                        s.block(n)
                        s.wait(gx_ready, PT)
                        s(nc.vector.tensor_scalar_add(gate[:, :, :], gate[:, :, :], 1.0))
                        s(nc.vector.reciprocal(gate[:, :, :], gate[:, :, :]))
                        for g in range(PT):
                            s(nc.vector.scalar_tensor_tensor(out=gate[:, g, :], in0=bank[2 + g // 2][:, (g % 2) * T1:(g % 2 + 1) * T1],
                                                             scalar=b1[:, PT + g:PT + g + 1], in1=gate[:, g, :],
                                                             op0=ALU.add, op1=ALU.mult), gate_ready)

                    def differences(n, first=False):
                        s.block(n)
                        if not first:
                            s.wait(pool_ps, 2, back=1)
                        lo = 16 if first else 0
                        for g in range(PT):
                            s.wait(win_ready, g + 1)
                            if first:
                                s(nc.vector.tensor_tensor(diff[:, g, 0:16], win[g][:, g, HALO:HALO + 16], inv_cnt[:, g, :], ALU.mult), diff_first)
                                s(nc.vector.tensor_tensor(diff[:, g, 0:16], diff[:, g, 0:16], u[:, g, HALO:HALO + 16], ALU.subtract), diff_first)
                            s(nc.vector.scalar_tensor_tensor(out=diff[:, g, lo:], in0=win[g][:, g, HALO + lo:], scalar=1.0 / WIN[g],
                                                             in1=u[:, g, HALO + lo:], op0=ALU.mult, op1=ALU.subtract), diff_ready)

                    def mixed(n):
                        s.block(n)
                        for b in range(2):
                            s.wait(pool_ps, b + 1)
                            s(nc.vector.tensor_tensor(yc[:, 2 * b:2 * b + 2, :].rearrange("p g t -> p (g t)"), bank[4 + b][:, :],
                                                      gate[:, 2 * b:2 * b + 2, :].rearrange("p g t -> p (g t)"), ALU.mult), yc_ready)

                    def residual(n):
                        s.block(n)
                        for j in range(2):
                            dve.wait_ge(xr_loaded[j], n * 16 + 16)
                            for h in range(2):
                                s.wait(out_ps, 2 * j + h + 1)
                                s(nc.vector.tensor_tensor(xr[:, j, h * 512:(h + 1) * 512], bank[6 + h][:, :],
                                                          xr[:, j, h * 512:(h + 1) * 512], ALU.add), h_ready)

                    gates(0)
                    differences(0, first=True)
                    mixed(0)
                    gates(1)
                    residual(0)
                    differences(1)
                    with dve.Fori(2, N1 - 1) as n:
                        mixed(n - 1)
                        gates(n)
                        residual(n - 1)
                        differences(n)
                    mixed(N1 - 2)
                    gates(N1 - 1)
                    residual(N1 - 2)
                    differences(N1 - 1)
                    mixed(N1 - 1)
                    residual(N1 - 1)

        with ExitStack() as st:
            def new(name, shape, dt=F32):
                return sb(name, shape, dt, stack=st)

            def signal(name, per, start=0):
                return Signal(sem(name, st), per, start)

            x_in = new("x2_in", [P, D])
            hr = new("hr", [P, D])
            junk = new("junk2", [P, D], BF16)
            stat = new("stat2", [P, 3])
            hstat = new("hstat", [P, 3])
            xT = new("xT2", [P, KT, T2])
            mix = new("mix", [P, MIX, T2])
            prev = new("prev", [P, MIX, 1 + T2])
            rg = new("rg", [P, NP, T2])
            rgate = new("rgate", [P, NP, T2])
            th = new("th", [P, T2])
            sig = new("sig", [P, 2, NP, T2])
            G = new("G", [P, NP, T2])
            egx = new("egx", [P, NP, T2])
            egi = new("egi", [P, NP, T2])
            kk = new("kk", [P, NP, T2])
            rn = new("rn", [P, NP, T2])
            t2 = new("t2", [P, NP, T2])
            k2 = new("k2", [P, NP, T2])
            rk = new("rk", [P, NP, T2])
            bonus = new("bonus", [P, NP, T2])
            LA = [new(f"LA{e}", [P, NP, NC, 2, C]) for e in range(2)]
            BK = new("BK", [P, NP, NC, 2, C])
            sm_of = [[new(f"SM{e}", [P, NP, 2, C]) for e in range(2)],
                     [t.rearrange("p a (b c) -> p a b c", b=2) for t in (rn[:, :, :], egx[:, :, :])]]
            SM = [[t[:] if j == 0 else t for t in sm_of[j]] for j in range(NC)]
            SV = [new(f"SV{e}", [P, NP, HD]) for e in range(2)]
            UV = [new(f"UV{e}", [P, NP, HD]) for e in range(2)]
            BT = [new(f"BT{e}", [P, NC, NP, HD]) for e in range(2)]
            DT = [new(f"DT{j}", [P, NP, P]) for j in range(NC)]
            ET = [new(f"ET{j}", [P, NP, P]) for j in range(NC)]
            Qx = [new(f"Qx{j}", [P, NP, P]) for j in range(NC)]
            Dx = [kk, t2]
            D2 = [k2, rk]
            Q1 = [new(f"Q1_{j}", [P, NP, HD]) for j in range(NC)]
            QD = [new(f"QD{j}", [P, NP, HD]) for j in range(NC)]
            Qr = [new(f"Qr{j}", [P, NP, HD]) for j in range(NC)]
            R = new("R", [P, NP, HD])
            Vt = new("Vt", [P, NC, NP, HD])
            Y = new("Y", [P, NP, T2])
            rs = new("rs", [P, NP, T2])
            stmp = new("stmp", [P, NP, HD])

            x_loaded, h_loaded, stored = sem("x2_loaded", st), sem("h_loaded", st), sem("stored", st)
            b2_ps, w2_ready, zero_ready, zero_link, set_link = (
                sem("b2_ps", st), sem("w2_ready", st), sem("zero_ready", st), sem("zero_link", st), sem("set_link", st))
            act_own = signal("act2_own", ACT_OWN)
            act_next = signal("act2_next", 3)
            dve_own = signal("dve2_own", DVE_OWN)
            pool_own = signal("pool2_own", 4 * NC + 1)
            xn_ready = signal("xn2_ready", 1)
            xT_ps = signal("xT2_ps", 2)
            xT_ready = signal("xT2_ready", 2)
            group_ps = signal("group_ps", 5)
            rg_ready = signal("rg_ready", NP)
            mix_in = signal("mix_in", 2 * MIX)
            mix_ready = signal("mix_ready", 4)
            carry_ready = signal("carry_ready", 1)
            eth_ready = signal("eth_ready", 1)
            k2_ready = signal("k2_ready", 1)
            th_ready = signal("th_ready", 1)
            lora_ps = signal("lora_ps", 2)
            e_ready = signal("e_ready", 2 * NP)
            clamp_ready = signal("clamp_ready", 3)
            ln_own = signal("ln_own", 3)
            sig_ready = signal("sig_ready", 3)
            G_ready = signal("G_ready", 1)
            gprev_ready = signal("gprev_ready", 1)
            exps_ready = signal("exps_ready", 3)
            kk_ready = signal("kk_ready", 1)
            kk2_ready = signal("kk2_ready", 1)
            norm_ps = signal("norm_ps", 1)
            rn_ready = signal("rn_ready", 1)
            rk_ready = signal("rk_ready", 1)
            bonus_ps = signal("bonus_ps", 1)
            erg_ready = signal("erg_ready", 1)
            rgate_ready = signal("rgate_ready", 1)
            prep_ready = signal("prep_ready", 1)
            kt_ready = signal("kt_ready", 1)
            gram_ps = signal("gram_ps", 2 * NC)
            vt_ps = signal("vt_ps", 1)
            bt_ps = signal("bt_ps", 1)
            inv_ps = signal("inv_ps", INV * NC)
            r_ps = signal("r_ps", NC)
            u_ps = signal("u_ps", NC)
            s_ps = signal("s_ps", NC)
            y_ps = signal("y_ps", NC)
            sm_ready = signal("sm_ready", 2 * NC)
            dt_ready = signal("dt_ready", NC)
            q1_ready = signal("q1_ready", NC)
            horner_ready = signal("horner_ready", 6 * NC)
            qd_ready = signal("qd_ready", NC)
            g_ready = signal("g_ready", 2 * NC)
            q_ready = signal("q_ready", NC)
            r_ready = signal("r_ready", NC)
            s_ready = signal("s_ready", NC)
            v_ready = signal("v_ready", 1)
            bt_ready = signal("bt_ready", 2)
            d_ready = signal("d_ready", NC)
            d2_ready = signal("d2_ready", NC)
            td_ready = signal("td_ready", NC)
            gt_ready = signal("gt_ready", NC)
            u_ready = signal("u2_ready", NC)
            y_ready = signal("y_ready", NC)
            et_ready = signal("et_ready", NC)
            la_ready = signal("la_ready", NC)
            sv_ready = signal("sv_ready", NC)
            uv_ready = signal("uv_ready", NC)
            ysq_ready = signal("ysq_ready", 1)
            var_ps = signal("var_ps", 1)
            rs_ready = signal("rs_ready", 1)
            y2_ready = signal("y2_ready", 1)
            out_ps = signal("out2_ps", 2)
            h_ready = signal("h2_ready", 2)
            hn_ready = signal("hn_ready", 1)
            hn_own = signal("hn_own", 2)
            out_ready = signal("out_ready", 1)

            GROUPS = [(13, 4), (0, 4), (4, 4), (12, 1), (8, 4)]
            SLOTS = [(gr, q, k) for gr, (_, n) in enumerate(GROUPS) for q in range(n) for k in (0, KT // 2)]

            x_t = A["x"][0].rearrange("(m p) d -> m p d", p=P)
            h1_t = h1.rearrange("(m p) d -> m p d", p=P)
            out_t = out[0].rearrange("(m p) d -> m p d", p=P)
            flat = "p a b -> p (a b)"

            def each_block(body):
                body(0, True, True)
                with body.eng.Fori(1, N2 - 1) as n:
                    body(n, False, True)
                body(N2 - 1, False, False)

            class Body:
                def __init__(self, eng, run):
                    self.eng, self.run = eng, run

                def __call__(self, n, first, more):
                    self.run(n, first, more)

            with nc.Block() as block:
                @block.sync
                def _(sp):
                    def step(n, ahead):
                        sp.dma_start(hr[:, :], rows_of(h1_t, n)).then_inc(h_loaded, 16)
                        if ahead:
                            sp.wait_ge(xT_ps.sem, xT_ps.at(n + 1, 2))
                            let_through(sp, sp_gate)
                            sp.dma_start(x_in[:, :], rows_of(x_t, n + 2)).then_inc(x_loaded, 16)
                        sp.wait_ge(out_ready.sem, out_ready.at(n, 1))
                        let_through(sp, sp_gate)
                        sp.dma_start(rows_of(out_t, n), hr[:, :]).then_inc(stored, 16)
                        sp.wait_ge(stored, n * 16 + 16)
                        let_through(sp, sp_gate)

                    sp.dma_start(x_in[:, :], x_t[0]).then_inc(x_loaded, 16)
                    sp.wait_ge(xT_ps.sem, xT_ps.at(0, 2))
                    sp.dma_start(x_in[:, :], x_t[1]).then_inc(x_loaded, 16)
                    with sp.Fori(0, N2 - 2) as n:
                        step(n, True)
                    step(N2 - 2, False)
                    step(N2 - 1, False)

                @block.tensor
                def _(pe):
                    s = Steps(pe, None)
                    nx = Steps(pe, None)
                    pv = Steps(pe, None)

                    pe.wait_ge(w2_loaded, 16 * (KT + 1))
                    for t in range(RT):
                        for k in range(KT):
                            last = nc.tensor.matmul(bank[7][:, t:t + 1], w2[:, k, t * P:(t + 1) * P], mod[:, k:k + 1],
                                                    start=(k == 0), stop=(k == KT - 1))
                    last.then_inc(b2_ps, 1)
                    pe.wait_ge(w2_ready, 1)
                    pe.wait_ge(zero_ready, 1)

                    def transposes(n):
                        nx.block(n)
                        nx.wait(xn_ready, 1)
                        for b in range(2):
                            if b:
                                nx.wait(xT_ready, 1)
                            for q in range(4):
                                k = 4 * b + q
                                last = nc.tensor.transpose(bank[0][:, q * P:(q + 1) * P], x_in[:, k * P:(k + 1) * P], ident[:, :])
                            last.then_inc(xT_ps.sem, 1)

                    def project(m):
                        gr, q, k0 = SLOTS[m]
                        if q == 0 and k0 == 0:
                            if gr < 2:
                                nx.wait(xT_ready, 2)
                            elif gr == 2:
                                nx.wait(rg_ready, NP)
                            elif gr == 3:
                                nx.wait(mix_in, 8)
                            else:
                                nx.wait(mix_in, 16)
                        t = GROUPS[gr][0] + q
                        for k in range(k0, k0 + KT // 2):
                            last = nc.tensor.matmul(bank[gr % 2][:, q * P:(q + 1) * P], w2[:, k, t * P:(t + 1) * P], xT[:, k, :],
                                                    start=(k == 0), stop=(k == KT - 1))
                        if q == GROUPS[gr][1] - 1 and k0:
                            last.then_inc(group_ps.sem, 1)

                    def out_half(h):
                        for p in range(NP):
                            last = nc.tensor.matmul(bank[1 - h][:, :], Y[:, p], wo2[:, p, h * 512:(h + 1) * 512],
                                                    start=(p == 0), stop=(p == NP - 1))
                        last.then_inc(out_ps.sem, 1)

                    def inverses(fill):
                        def full(j, lhsT, rhs):
                            for p in range(NP):
                                last = nc.tensor.matmul(bank[2 + j][:, p * P:(p + 1) * P], lhsT[:, p], rhs[:, p], start=True, stop=True)
                            last.then_inc(inv_ps.sem, 1)

                        def turn(j, t):
                            for p in range(NP):
                                last = nc.tensor.transpose(bank[2 + j][:, p * P:(p + 1) * P], t[:, p], ident[:, :])
                            last.then_inc(inv_ps.sem, 1)

                        def apply(j, i, lhsT, rhs):
                            o = (i % 2) * 256
                            for p in range(NP):
                                last = nc.tensor.matmul(bank[2 + j][:, o + p * HD:o + (p + 1) * HD], lhsT[:, p], rhs[:, p],
                                                        start=True, stop=True)
                            last.then_inc(inv_ps.sem, 1)

                        for j in range(NC):
                            s.wait(dt_ready, j + 1)
                            turn(j, DT[j])
                        fill()
                        for j in range(NC):
                            s.wait(d_ready, j + 1)
                            full(j, DT[j], Dx[j])
                        fill()
                        for i in range(7):
                            for j in range(NC):
                                if i:
                                    s.wait(horner_ready, NC * (i - 1) + j + 1)
                                else:
                                    s.wait(d2_ready, j + 1)
                                    s.wait(q1_ready, j + 1)
                                apply(j, i, D2[j], Qr[j] if i else Q1[j])
                            fill()
                        for j in range(NC):
                            s.wait(qd_ready, j + 1)
                            turn(j, Qx[j])
                        fill()
                        for j in range(NC):
                            s.wait(td_ready, j + 1)
                            s.wait(et_ready, j + 1)
                            full(j, ET[j], Dx[j])
                        fill()
                        for i in range(3):
                            for j in range(NC):
                                if i:
                                    s.wait(g_ready, NC * (i - 1) + j + 1)
                                else:
                                    s.wait(gt_ready, j + 1)
                                apply(j, i, D2[j], Qr[j] if i else QD[j])
                            fill()

                    def chain(j, fill):
                        s.wait(sv_ready, j + 1)
                        s.wait(la_ready, j + 1)
                        if j:
                            s.wait(s_ready, j)
                        for p in range(NP):
                            for e in range(2):
                                last = nc.tensor.matmul(bank[5][half(e), p * HD:(p + 1) * HD], LA[e][:, p, j, 0], SV[e][:, p],
                                                        start=True, stop=True)
                        last.then_inc(r_ps.sem, 1)
                        fill()
                        s.wait(q_ready, j + 1)
                        s.wait(r_ready, j + 1)
                        for p in range(NP):
                            last = nc.tensor.matmul(bank[5][:, 256 + p * HD:256 + (p + 1) * HD], Qx[j][:, p], R[:, p], start=True, stop=True)
                        last.then_inc(u_ps.sem, 1)
                        fill()
                        s.wait(uv_ready, j + 1)
                        s.wait(u_ready, j + 1)
                        for p in range(NP):
                            for e in range(2):
                                last = nc.tensor.matmul(bank[7][half(e), p * HD:(p + 1) * HD], BT[e][:, j, p], UV[e][:, p],
                                                        start=True, stop=True)
                        last.then_inc(s_ps.sem, 1)
                        if j:
                            s.wait(y_ready, j)
                        for p in range(NP):
                            for e in range(2):
                                o = bank[6][half(e), p * HD:(p + 1) * HD]
                                nc.tensor.matmul(o, UV[e][:, p], SM[j][e][:, p, 1], start=True, stop=False)
                                last = nc.tensor.matmul(o, SV[e][:, p], LA[e][:, p, j, 1], start=False, stop=True)
                        last.then_inc(y_ps.sem, 1)
                        fill()

                    def run(n, first, more):
                        s.block(n)
                        if not first:
                            pv.block(n - 1)
                        m = [0]

                        def fill():
                            if more and m[0] < len(SLOTS):
                                project(m[0])
                                m[0] += 1

                        s.wait(mix_ready, 4)
                        s.wait(th_ready, 1)
                        for i, (part, rhs) in enumerate(((slice(0, LORA), th[0:LORA, :]), (slice(LORA, P), mix[LORA:P, 12, :]))):
                            for p in range(NP):
                                last = nc.tensor.matmul(bank[2 + i][:, p * P:(p + 1) * P], up[part, p * P:(p + 1) * P], rhs,
                                                        start=True, stop=True)
                            last.then_inc(lora_ps.sem, 1)
                        if not first:
                            pv.wait(y2_ready, 1)
                            out_half(0)
                        s.wait(kk2_ready, 1)
                        nc.tensor.matmul(bank[5][:, :], head_sum[:, :], rn[:, :, :].rearrange(flat), start=True, stop=True)\
                            .then_inc(norm_ps.sem, 1)
                        if not first:
                            out_half(1)
                        s.wait(rk_ready, 1)
                        for p in range(NP):
                            last = nc.tensor.matmul(bank[6][:, p * P:(p + 1) * P], rk_sum[:, p], rk[:, p], start=True, stop=True)
                        last.then_inc(bonus_ps.sem, 1)
                        s.wait(kt_ready, 1)
                        s.wait(prep_ready, 1)
                        for j in range(NC):
                            for e in range(2):
                                for p in range(NP):
                                    last = nc.tensor.matmul(bank[((2, 3), (4, 7))[j][e]][:, p * P:(p + 1) * P], BK[half(e), p, j].rearrange(flat),
                                                            LA[e][half(e), p, j].rearrange(flat), start=True, stop=True)
                                last.then_inc(gram_ps.sem, 1)
                        s.wait(rn_ready, 1)
                        if not first:
                            pv.wait(h_ready, 2)
                        for j in range(NC):
                            for p in range(NP):
                                for e in range(2):
                                    o = j * 256 + p * HD
                                    last = nc.tensor.matmul(bank[5][half(1 - e), o:o + HD], mix[:, 8 + p, j * C:(j + 1) * C],
                                                            center[:, half(e)], start=True, stop=True)
                        last.then_inc(vt_ps.sem, 1)
                        for e in range(2):
                            for j in range(NC):
                                for p in range(NP):
                                    o = j * 256 + p * HD
                                    last = nc.tensor.transpose(bank[(6, 1)[e]][:, o:o + HD], BK[half(e), p, j].rearrange(flat),
                                                               ident[half(e), half(e)])
                        last.then_inc(bt_ps.sem, 1)
                        if more:
                            transposes(n + 1)
                        inverses(fill)
                        chain(0, fill)
                        fill()
                        chain(1, fill)
                        for _ in range(4):
                            fill()
                        s.wait(ysq_ready, 1)
                        nc.tensor.matmul(bank[4][:, :], head_mean[:, :], rs[:, :, :].rearrange(flat), start=True, stop=True)\
                            .then_inc(var_ps.sem, 1)
                        while more and m[0] < len(SLOTS):
                            fill()

                    transposes(0)
                    for m in range(len(SLOTS)):
                        project(m)
                    each_block(Body(pe, run))
                    pv.block(N2 - 1)
                    pv.wait(y2_ready, 1)
                    out_half(0)
                    out_half(1)

                @block.scalar
                def _(act):
                    s = Steps(act, act_own)
                    nx = Steps(act, act_next)
                    pv = Steps(act, hn_own)

                    def norm(n):
                        nx.block(n)
                        act.wait_ge(x_loaded, n * 16 + 16)
                        nx(nc.scalar.activation(junk[:, :], x_in[:, :], ACT.Square, accum_out=stat[:, 0:1]))
                        nx(nc.scalar.activation(stat[:, 1:2], stat[:, 0:1], ACT.Ln, scale=1.0 / D, bias=eps[:, 0:1]))
                        nx(nc.scalar.activation(stat[:, 2:3], stat[:, 1:2], ACT.Exp, scale=-0.5))
                        nx(nc.scalar.activation(x_in[:, :], x_in[:, :], ACT.Copy, scale=stat[:, 2:3]), xn_ready)

                    def take_xT():
                        for b in range(2):
                            nx.wait(xT_ps, b + 1)
                            nx(nc.scalar.activation(xT[:, 4 * b:4 * b + 4, :].rearrange(flat), bank[0][:, :], ACT.Copy), xT_ready)

                    def take_group(gr):
                        t0, w = GROUPS[gr]
                        nx.wait(group_ps, gr + 1)
                        for q in range(w):
                            src = bank[gr % 2][:, q * P:(q + 1) * P]
                            t = t0 + q
                            if gr == 0:
                                nx(nc.scalar.activation(rg[:, q], src, ACT.Identity, bias=b2[:, t:t + 1]), rg_ready, hold=False)
                            else:
                                nx(nc.scalar.activation(mix[:, t], src, ACT.Identity, scale=omu[:, t:t + 1], bias=omub[:, t:t + 1]), mix_in,
                                   hold=False)
                                nx(nc.scalar.activation(prev[:, t, 1:], src, ACT.Identity, scale=v("mu", t), bias=mub[:, t:t + 1]), mix_in,
                                   hold=False)

                    def sigmoid(i, t):
                        s.wait(clamp_ready, i + 1)
                        s(nc.scalar.activation(t, t, ACT.Ln, bias=1.0), ln_own)
                        s(nc.scalar.activation(t, t, ACT.Exp, scale=-1.0), sig_ready)

                    def residual_norm(n):
                        pv.block(n)
                        pv.wait(h_ready, 2)
                        pv(nc.scalar.activation(junk[:, :], hr[:, :], ACT.Square, accum_out=hstat[:, 0:1]))
                        pv(nc.scalar.activation(hstat[:, 1:2], hstat[:, 0:1], ACT.Ln, scale=1.0 / D, bias=eps[:, 0:1]))
                        pv(nc.scalar.activation(hstat[:, 2:3], hstat[:, 1:2], ACT.Exp, scale=-0.5), hn_ready)

                    def run(n, first, more):
                        s.block(n)
                        s.wait(mix_ready, 4)
                        s(nc.scalar.activation(th[0:LORA, :], mix[0:LORA, 12, :], ACT.Exp, scale=-2.0), eth_ready)
                        s.wait(kk_ready, 1)
                        s(nc.scalar.activation(rgate[:, :, :], rg[:, :, :], ACT.Exp, scale=-1.0), erg_ready)
                        for i in range(2):
                            s.wait(lora_ps, i + 1)
                            for p in range(NP):
                                s(nc.scalar.activation(sig[:, i, p], bank[2 + i][:, p * P:(p + 1) * P], ACT.Exp, scale=-1.0,
                                                       bias=negv[:, i, p:p + 1]), e_ready, hold=False)
                        sigmoid(0, sig[:, 0])
                        sigmoid(1, sig[:, 1])
                        s.wait(norm_ps, 1)
                        s(nc.scalar.activation(rn[:, :, :].rearrange(flat), bank[5][:, :], ACT.Ln, bias=eps[:, 1:2]))
                        s(nc.scalar.activation(rn[:, :, :], rn[:, :, :], ACT.Exp, scale=-0.5), rn_ready)
                        s.wait(G_ready, 1)
                        s(nc.scalar.activation(egi[:, :, :], G[:, :, :], ACT.Exp, scale=DECAY), exps_ready)
                        s.wait(gprev_ready, 1)
                        s(nc.scalar.activation(sig[:, 0], G[:, :, :], ACT.Exp, scale=-DECAY), exps_ready)
                        s(nc.scalar.activation(egx[:, :, :], egx[:, :, :], ACT.Exp, scale=-DECAY), exps_ready)
                        sigmoid(2, rgate[:, :, :])
                        if not first:
                            residual_norm(n - 1)
                        if more:
                            norm(n + 1)
                        s.wait(vt_ps, 1)
                        s(nc.scalar.activation(Vt[:, :, :, :].rearrange("p j a b -> p (j a b)"), bank[5][:, :], ACT.Copy), v_ready)
                        s.wait(bt_ps, 1)
                        for e in range(2):
                            s(nc.scalar.activation(BT[e][:, :, :, :].rearrange("p j a b -> p (j a b)"), bank[(6, 1)[e]][:, :], ACT.Copy), bt_ready)
                        if more:
                            take_xT()
                        for j in range(NC):
                            s.wait(inv_ps, j + 1)
                            s(nc.scalar.activation(Dx[j][:, :, :].rearrange(flat), bank[2 + j][:, :], ACT.Copy), d_ready)
                        for j in range(NC):
                            s.wait(inv_ps, NC + j + 1)
                            s(nc.scalar.activation(D2[j][:, :, :].rearrange(flat), bank[2 + j][:, :], ACT.Copy), d2_ready)
                        if more:
                            take_group(0)
                        for j in range(NC):
                            s.wait(inv_ps, NC * 9 + j + 1)
                            s(nc.scalar.activation(Dx[j][:, :, :].rearrange(flat), bank[2 + j][:, :], ACT.Copy), td_ready)
                        for j in range(NC):
                            s.wait(inv_ps, NC * 10 + j + 1)
                            s(nc.scalar.activation(D2[j][:, :, :].rearrange(flat), bank[2 + j][:, :], ACT.Copy), gt_ready)
                        if more:
                            s.wait(carry_ready, 1)
                            take_group(1)
                        for j in range(NC):
                            s.wait(u_ps, j + 1)
                            if j:
                                s.wait(y_ps, j)
                            s(nc.scalar.activation(UV[0][half(0), :, :].rearrange(flat), bank[5][half(0), 256:512], ACT.Copy), hold=False)
                            s(nc.scalar.activation(UV[1][half(1), :, :].rearrange(flat), bank[5][half(1), 256:512], ACT.Copy), u_ready)
                            if more and j:
                                take_group(2)
                            s.wait(y_ps, j + 1)
                            s(nc.scalar.activation(Y[:, :, j * C:(j + 1) * C], bank[6][:, 0:256].rearrange("p (a b) -> p a b", b=C),
                                                   ACT.Copy), y_ready)
                        s(nc.scalar.activation(rs[:, :, :], Y[:, :, :], ACT.Square), ysq_ready)
                        if more:
                            take_group(3)
                        s.wait(var_ps, 1)
                        s(nc.scalar.activation(rs[:, :, :].rearrange(flat), bank[4][:, :], ACT.Ln, bias=eps[:, 2:3]))
                        s(nc.scalar.activation(rs[:, :, :], rs[:, :, :], ACT.Exp, scale=-0.5), rs_ready)
                        if more:
                            take_group(4)
                        s.end("act")

                    nc.scalar.preload_act_table_set("natural_log_exp_and_others")
                    act.wait_ge(w2_ready, 1)
                    act.wait_ge(zero_ready, 1)
                    norm(0)
                    take_xT()
                    for gr in range(5):
                        take_group(gr)
                    each_block(Body(act, run))
                    residual_norm(N2 - 1)

                @block.gpsimd
                def _(pool):
                    s = Steps(pool, pool_own)
                    nx = Steps(pool, pool_own)

                    def copy(to, of, one):
                        return nc.gpsimd.tensor_tensor(to, of, one, ALU.mult)

                    def ones_of(part):
                        return ones[part, :].unsqueeze(1).broadcast_to([HD, NP, HD])

                    def carry(n):
                        nx.block(n)
                        nx.wait(mix_ready, 4)
                        nx(copy(prev[:, :, 0:1], prev[:, :, T2:T2 + 1], ones[:, 0:MIX].unsqueeze(2)), carry_ready)

                    def run(n, first, more):
                        s.block(n)
                        s.wait(kk_ready, 1)
                        s(nc.gpsimd.tensor_tensor(rn[:, :, :], kk[:, :, :], kk[:, :, :], ALU.mult), kk2_ready)
                        s.wait(G_ready, 1)
                        s(nc.gpsimd.tensor_tensor(egx[:, :, :], G[:, :, :], sig[:, 0], ALU.subtract), gprev_ready)
                        s.wait(k2_ready, 1)
                        s.wait(exps_ready, 1)
                        for e in range(2):
                            h = half(e)
                            s(nc.gpsimd.tensor_tensor(BK[h, :, :, 1 - e], chunks(k2[h]), chunks(egi[h]), ALU.mult),
                              kt_ready if e else pool_own)
                        for j in range(NC):
                            for e in range(2):
                                s.wait(sm_ready, 2 * j + e + 1)
                                s(nc.gpsimd.tensor_tensor(ET[j][half(e), :, half(e)], SM[j][e][half(e), :, 0],
                                                          off16[half(e), :].unsqueeze(1).broadcast_to([HD, NP, HD]), ALU.mult),
                                  et_ready if e else pool_own)
                            for e in range(2):
                                o = half(1 - e)
                                s(copy(LA[e][o, :, j, 0], SM[j][e][o, :, 0], ones_of(o)), la_ready if e else pool_own)
                        s.wait(v_ready, 1)
                        for j in range(NC):
                            if j:
                                s.wait(y_ps, j)
                            for e in range(2):
                                o = half(1 - e)
                                s(copy(SV[e][o], Vt[o, j], ones_of(o)), sv_ready if e else pool_own)
                            for e in range(2):
                                o = half(1 - e)
                                s(copy(UV[e][o], Vt[o, j], ones_of(o)), uv_ready if e else pool_own)
                        if more:
                            carry(n + 1)
                        s.end("pool")

                    k = 0
                    for t in [*LA, *DT, *ET, *Qx, *SV]:
                        k += 1
                        nc.gpsimd.memset(t[:], 0.0).then_inc(zero_link, 1)
                        pool.wait_ge(zero_link, k)
                    nc.gpsimd.memset(prev[:, :, 0:1], 0.0).then_inc(zero_ready, 1)
                    pool.wait_ge(zero_ready, 1)
                    carry(0)
                    each_block(Body(pool, run))

                @block.vector
                def _(dve):
                    s = Steps(dve, dve_own)
                    nx = Steps(dve, None)
                    pv = Steps(dve, None)

                    def shift(n, i):
                        nx.block(n)
                        t0, w = GROUPS[i + 1]
                        nx.count[mix_ready] = i
                        nx.wait(mix_in, (8, 16, 18, 26)[i])
                        nx(nc.vector.tensor_tensor(mix[:, t0:t0 + w, :], mix[:, t0:t0 + w, :], prev[:, t0:t0 + w, 0:T2], ALU.add), mix_ready)

                    def clamp(t, i):
                        s(nc.vector.tensor_scalar(t, t, LN_MAX, None, ALU.min), clamp_ready)

                    def residual(n, h):
                        pv.block(n)
                        pv.count[h_ready] = h
                        if h == 0:
                            dve.wait_ge(h_loaded, n * 16 + 16)
                        pv.wait(out_ps, h + 1)
                        pv(nc.vector.tensor_tensor(hr[:, h * 512:(h + 1) * 512], bank[1 - h][:, :], hr[:, h * 512:(h + 1) * 512], ALU.add), h_ready)

                    def final_norm(n):
                        pv.block(n)
                        pv.wait(hn_ready, 1)
                        pv(nc.vector.scalar_tensor_tensor(out=hr[:, :], in0=hr[:, :], scalar=hstat[:, 2:3], in1=fgain[:, :],
                                                          op0=ALU.mult, op1=ALU.mult), out_ready)

                    def per_head(t):
                        return t.rearrange("p (a b) -> p a b", b=HD)

                    def run(n, first, more):
                        s.block(n)
                        s.wait(eth_ready, 1)
                        s(nc.vector.tensor_scalar_add(th[0:LORA, :], th[0:LORA, :], 1.0))
                        s(nc.vector.reciprocal(th[0:LORA, :], th[0:LORA, :]))
                        s(nc.vector.tensor_scalar(th[0:LORA, :], th[0:LORA, :], 2.0, -1.0, ALU.mult, ALU.add), th_ready)
                        s(nc.vector.tensor_tensor(kk[:, :, :], mix[:, 4:8, :], wide(v("k_k", 0, NP)), ALU.mult), kk_ready)
                        s.wait(e_ready, NP)
                        clamp(sig[:, 0], 0)
                        s.wait(e_ready, 2 * NP)
                        clamp(sig[:, 1], 1)
                        s.wait(erg_ready, 1)
                        clamp(rgate[:, :, :], 2)
                        s.wait(sig_ready, 1)
                        s(nc.vector.tensor_tensor_scan(G[:, :, :].rearrange(flat), restart[:, :], sig[:, 0].rearrange(flat), 0.0,
                                                       ALU.mult, ALU.add), G_ready)
                        s.wait(sig_ready, 2)
                        for p in range(NP):
                            s(nc.vector.tensor_scalar(t2[:, p], sig[:, 1, p], v("k_a", p), oka[:, p:p + 1], ALU.mult, ALU.add), hold=(p == NP - 1))
                        s(nc.vector.tensor_tensor(k2[:, :, :], mix[:, 4:8, :], t2[:, :, :], ALU.mult), k2_ready)
                        s(nc.vector.tensor_tensor(rk[:, :, :], mix[:, 0:4, :], k2[:, :, :], ALU.mult), rk_ready)
                        if not first:
                            residual(n - 1, 0)
                        s.wait(rn_ready, 1)
                        s(nc.vector.tensor_tensor(kk[:, :, :], kk[:, :, :], rn[:, :, :], ALU.mult))
                        s(nc.vector.scalar_tensor_tensor(out=t2[:, :, :], in0=kk[:, :, :], scalar=-1.0, in1=sig[:, 1],
                                                         op0=ALU.mult, op1=ALU.mult))
                        s.wait(exps_ready, 1)
                        for e in range(2):
                            h = half(e)
                            s(nc.vector.tensor_tensor(BK[h, :, :, e], chunks(t2[h]), chunks(egi[h]), ALU.mult), hold=False)
                        s.wait(exps_ready, 2)
                        for e in range(2):
                            h = half(e)
                            s(nc.vector.tensor_tensor(LA[e][h, :, :, 1], chunks(mix[h, 0:4]), chunks(sig[h, 0]), ALU.mult), hold=False)
                        s.wait(exps_ready, 3)
                        for e in range(2):
                            h = half(e)
                            s(nc.vector.tensor_tensor(LA[e][h, :, :, 0], chunks(kk[h]), chunks(egx[h]), ALU.mult), hold=False)
                        s.wait(bonus_ps, 1)
                        s(nc.vector.tensor_tensor(bonus[:, :, :].rearrange(flat), bank[6][:, :], mix[:, 8:12, :].rearrange(flat), ALU.mult),
                          prep_ready)
                        s.wait(sig_ready, 3)
                        s(nc.vector.tensor_tensor(rgate[:, :, :], rgate[:, :, :], rg[:, :, :], ALU.mult), rgate_ready)
                        if not first:
                            residual(n - 1, 1)
                        s.wait(kt_ready, 1)
                        for j in range(NC):
                            for e in range(2):
                                s.wait(gram_ps, 2 * j + e + 1)
                                s(nc.vector.tensor_tensor(SM[j][e].rearrange("p a b c -> p a (b c)"),
                                                          bank[((2, 3), (4, 7))[j][e]][:, :].rearrange("p (a b) -> p a b", b=P),
                                                          gram_mask[:, :].unsqueeze(1).broadcast_to([P, NP, P]), ALU.mult), sm_ready)
                            for e in range(2):
                                h = half(e)
                                s(nc.vector.tensor_tensor(DT[j][h, :, h], SM[j][e][h, :, 0],
                                                          diag16[h, :].unsqueeze(1).broadcast_to([HD, NP, HD]), ALU.mult),
                                  dt_ready if e else None, hold=bool(e))
                        for j in range(NC):
                            for e in range(2):
                                h = half(e)
                                s(nc.vector.tensor_tensor(Q1[j][h], DT[j][h, :, h],
                                                          ident64[h, :].unsqueeze(1).broadcast_to([HD, NP, HD]), ALU.add),
                                  q1_ready if e else None, hold=bool(e))
                        if not first:
                            final_norm(n - 1)
                        for i in range(6):
                            for j in range(NC):
                                s.wait(inv_ps, NC * (2 + i) + j + 1)
                                s(nc.vector.tensor_tensor(Qr[j][:, :, :].rearrange(flat), bank[2 + j][:, (i % 2) * 256:(i % 2) * 256 + 256],
                                                          Q1[j][:, :, :].rearrange(flat), ALU.add), horner_ready, hold=False)
                        for j in range(NC):
                            s.wait(inv_ps, NC * 8 + j + 1)
                            s(nc.vector.tensor_tensor(QD[j][:, :, :].rearrange(flat), bank[2 + j][:, 0:256],
                                                      Q1[j][:, :, :].rearrange(flat), ALU.add))
                            for e in range(2):
                                s(nc.vector.tensor_copy(Qx[j][half(e), :, half(e)], QD[j][half(e)]), qd_ready if e else None, hold=bool(e))
                        for i in range(2):
                            for j in range(NC):
                                s.wait(inv_ps, NC * (11 + i) + j + 1)
                                s(nc.vector.tensor_tensor(Qr[j][:, :, :].rearrange(flat), bank[2 + j][:, i * 256:i * 256 + 256],
                                                          QD[j][:, :, :].rearrange(flat), ALU.add), g_ready, hold=False)
                        for j in range(NC):
                            s.wait(inv_ps, NC * 13 + j + 1)
                            for e in range(2):
                                h = half(e)
                                s(nc.vector.tensor_tensor(Qx[j][h, :, h], per_head(bank[2 + j][h, 0:256]), QD[j][h], ALU.add),
                                  q_ready if e else None, hold=bool(e))
                        for j in range(NC):
                            s.wait(r_ps, j + 1)
                            s(nc.vector.tensor_copy(R[:, :, :].rearrange(flat), bank[5][:, 0:256]), r_ready)
                            if more and j == 0:
                                shift(n + 1, 0)
                            s.wait(y_ps, j + 1)
                            last = C * (j + 1) - 1
                            for e in range(2):
                                h = half(e)
                                s(nc.vector.tensor_tensor(stmp[h], per_head(bank[7][h, 0:256]), SV[e][h], ALU.add), hold=bool(e))
                            for e in range(2):
                                h = half(e)
                                s(nc.vector.tensor_tensor(SV[e][h], stmp[h], sig[h, 0, :, last:last + 1].broadcast_to([HD, NP, HD]), ALU.mult),
                                  s_ready if e else None, hold=bool(e))
                        if more:
                            shift(n + 1, 1)
                            shift(n + 1, 2)
                        s.wait(y_ready, NC)
                        s.wait(rs_ready, 1)
                        s(nc.vector.tensor_tensor(Y[:, :, :], Y[:, :, :], rs[:, :, :], ALU.mult))
                        for p in range(NP):
                            s(nc.vector.tensor_scalar(Y[:, p], Y[:, p], v("lnx_w", p), v("lnx_b", p), ALU.mult, ALU.add), hold=(p == NP - 1))
                        s(nc.vector.tensor_tensor(Y[:, :, :], Y[:, :, :], bonus[:, :, :], ALU.add))
                        s(nc.vector.tensor_tensor(Y[:, :, :], Y[:, :, :], rgate[:, :, :], ALU.mult), y2_ready)
                        if more:
                            shift(n + 1, 3)
                        s.end("dve")

                    dve.wait_ge(b2_ps, 1)
                    k = [0]

                    def link(ins):
                        k[0] += 1
                        ins.then_inc(set_link, 1)
                        dve.wait_ge(set_link, k[0])

                    link(nc.vector.tensor_copy(b2[:, :], bank[7][:, 0:RT]))
                    link(nc.vector.tensor_tensor(omub[:, :], b2[:, 0:MIX], omu[:, :], ALU.mult))
                    link(nc.vector.tensor_tensor(mub[:, :], b2[:, 0:MIX], v("mu", 0, MIX), ALU.mult))
                    for t in range(KT):
                        link(nc.vector.tensor_scalar(w2[:, t, :], w2[:, t, :], gsc[:, t:t + 1], None, ALU.mult))
                    for t in range(NP - 1):
                        link(nc.vector.tensor_tensor(wo2[:, t, :], wo2[:, t, :], gate_row[:, :], ALU.mult))
                    nc.vector.tensor_tensor(wo2[:, NP - 1, :], wo2[:, NP - 1, :], gate_row[:, :], ALU.mult).then_inc(w2_ready, 1)
                    dve.wait_ge(zero_ready, 1)
                    for i in range(4):
                        shift(0, i)
                    each_block(Body(dve, run))
                    residual(N2 - 1, 0)
                    residual(N2 - 1, 1)
                    final_norm(N2 - 1)


_INS = ["x", "c", "w_ada", "b_ada", "norm_gain", "w_in", "pool_w", "pool_scale", "mu", "w0", "w_lora_up", "a0",
        "a_lora_up", "k_k", "k_a", "r_k", "lnx_w", "lnx_b", "w_out", "final_gain"]


def kernel(**inputs):
    import numpy as np
    import concourse.bacc as bacc
    from concourse import mybir as _mybir
    from concourse.bass_utils import run_bass_kernel_spmd

    nc = bacc.Bacc("TRN2", target_bir_lowering=False, num_devices=1)
    arrays, args = {}, {}
    for name in _INS:
        a = np.ascontiguousarray(inputs[name])
        arrays[f"in_{name}"] = a
        args[name] = nc.dram_tensor(f"in_{name}", a.shape, _mybir.dt.from_np(a.dtype), kind="ExternalInput").ap()
    out = nc.dram_tensor("out_0", (1, SEQ, D), F32, kind="ExternalOutput").ap()
    build(nc, args, out)
    r = run_bass_kernel_spmd(nc, [arrays], core_ids=[0])
    return r.results[0]["out_0"]
```

```python
from contextlib import ExitStack
import math

import concourse.bass as bass
from concourse import mybir

F32 = mybir.dt.float32
BF16 = mybir.dt.bfloat16
ALU = mybir.AluOpType
ACT = mybir.ActivationFunctionType
AX = mybir.AxisListType

P = 128
D = 1024
KT = D // P
SEQ = 4096
POOLW = 512
PT = POOLW // P
RW = 512
NP = RW // P
HD = 64
LORA = 64
WIN = (2, 4, 8, 16)
HALO = 15
EPS = 1e-6
GN_EPS = 64e-5
KK_EPS = 1e-12
DECAY = math.exp(-0.5)

T1 = 256
N1 = SEQ // T1
T2 = 128
N2 = SEQ // T2
C = 64
NC = T2 // C
MIX = 13
POOL_COLS = 2 * POOLW
R_COLS = MIX * P + RW
RT = R_COLS // P
INV = 14
HEAD_DVE = 10
DVE_OWN = 20
LN_MAX = 1e19

ROWS = {}
for _n, _k in (("b_ada", 24), ("norm_gain", 8), ("mu", 13), ("pool_scale", 4), ("w0", 4), ("a0", 4),
               ("k_k", 4), ("k_a", 4), ("r_k", 4), ("lnx_w", 4), ("lnx_b", 4), ("c", 8)):
    ROWS[_n] = (sum(k for _, k in ROWS.values()), _k)
NROWS = sum(k for _, k in ROWS.values())


class Signal:

    def __init__(self, sem, per, start=0):
        self.sem, self.per, self.start = sem, per, start

    def at(self, n, k):
        return n * self.per + (self.start + k)


class Steps:

    def __init__(self, eng, own):
        self.eng, self.own = eng, own

    def block(self, n):
        self.n, self.count = n, {}

    def __call__(self, ins, signal=None, hold=True):
        s = signal or self.own
        self.count[s] = self.count.get(s, 0) + 1
        ins.then_inc(s.sem, 1)
        if hold:
            self.eng.wait_ge(s.sem, s.at(self.n, self.count[s]))

    def wait(self, signal, k, back=0):
        self.eng.wait_ge(signal.sem, signal.at(self.n, k - back * signal.per))

    def end(self, name, full=True):
        for s, k in self.count.items():
            if full:
                assert k == s.per, (name, s.sem.name, k, s.per)


def rows_of(view, n):
    if isinstance(n, int):
        return view[n]
    part = view[bass.ds(n, 1)]
    return part.rearrange("a p d -> (a p) d") if len(part.shape) == 3 else part.rearrange("a p j d -> (a p) j d")


def let_through(sp, gate):
    sp.sem_inc(gate, 1)


def wide(v):
    return v.unsqueeze(2).broadcast_to([P, NP, T2])


def chunks(t):
    return t.rearrange("p a (c t) -> p a c t", t=C)


def half(e):
    return slice(HD * e, HD * e + HD)


def build(nc, A, out):
    h1 = nc.dram_tensor("h1_dram", (SEQ, D), F32, kind="Internal").ap()
    ctx = ExitStack()
    with ctx:
        def sb(name, shape, dt=F32, stack=ctx):
            return stack.enter_context(nc.sbuf_tensor(name, shape, dt))

        def sem(name, stack=ctx):
            return stack.enter_context(nc.semaphore(name))

        bank = [ctx.enter_context(nc.psum_tensor(f"bank{b}", [P, 512], F32)) for b in range(8)]

        w2 = sb("w2", [P, KT, R_COLS])
        wo2 = sb("wo2", [P, NP, D])
        up = sb("up", [P, RW])
        ident = sb("ident", [P, P])
        center = sb("center", [P, P])
        head_mean = sb("head_mean", [P, P])
        head_sum = sb("head_sum", [P, P])
        rk_sum = sb("rk_sum", [P, NP, P])
        gram_mask = sb("gram_mask", [P, P])
        diag16 = sb("diag16", [P, HD])
        off16 = sb("off16", [P, HD])
        ident64 = sb("ident64", [P, HD])
        ones = sb("ones", [P, HD])
        restart = sb("restart", [P, NP * T2])
        fgain = sb("fgain", [P, D])
        gate_row = sb("gate_row", [P, D])
        rows = sb("rows", [P, P])
        vec = sb("vec", [P, NROWS])
        mod = sb("mod", [P, 16])
        gsc = sb("gsc", [P, KT])
        sc = sb("sc", [P, 3, KT])
        omu = sb("omu", [P, MIX])
        negv = sb("negv", [P, 2, NP])
        oka = sb("oka", [P, NP])
        eps = sb("eps", [P, 3])

        def v(name, t=0, n=1):
            return vec[:, ROWS[name][0] + t:ROWS[name][0] + t + n]

        pass1 = ExitStack()
        w1 = sb("w1", [P, KT, POOL_COLS], stack=pass1)
        wo1 = sb("wo1", [P, PT, D], stack=pass1)
        poolw = sb("poolw", [P, PT, P], stack=pass1)

        w2_loaded = sem("w2_loaded")
        sp_gate = sem("sp_gate")
        w_in_v = A["w_in"][0].rearrange("(k p) n -> p k n", p=P)
        w_out_v = A["w_out"][0].rearrange("(k p) n -> p k n", p=P)

        with ExitStack() as st:
            stage = sb("stage", [P, 3, KT, P], stack=st)
            bgate = sb("bgate", [P, D], stack=st)
            rows_in, w_in1, small_in = sem("rows_in", st), sem("w_in1", st), sem("small_in", st)
            staged = [sem(f"staged{j}", st) for j in range(3)]
            used = sem("stage_used", st)
            consts, vec_ps, vec_ok = sem("consts", st), sem("vec_ps", st), sem("vec_ok", st)
            sc_exp, sc_ok, mod_ps = sem("sc_exp", st), sem("sc_ok", st), sem("mod_ps", st)
            mod_ok, dve_link, pool_link = (sem("mod_ok", st), sem("dve_link", st),
                                                  sem("pool_link", st))
            ada = A["w_ada"][0].rearrange("(k p) n -> p k n", p=P)
            flat = {"r_k": A["r_k"][0].rearrange("h d -> (h d)"), "c": A["c"][0]}

            with nc.Block() as block:
                @block.sync
                def _(sp):
                    for j in range(3):
                        sp.dma_start(stage[:, j], ada[:, :, j * P:(j + 1) * P]).then_inc(staged[j], 16)
                    for name, (r0, k) in ROWS.items():
                        src = flat[name] if name in flat else A[name][0]
                        sp.dma_start(rows[r0:r0 + k, :], src.rearrange("(k p) -> k p", p=P)).then_inc(rows_in, 16)
                    for j in range(3, 24):
                        sp.wait_ge(used, j - 2)
                        sp.dma_start(stage[:, j % 3], ada[:, :, j * P:(j + 1) * P]).then_inc(staged[j % 3], 16)

                @block.scalar
                def _(act):
                    act.dma_start(bgate[:, :], A["b_ada"][:, 2 * D:3 * D].partition_broadcast(P)).then_inc(small_in, 16)
                    act.dma_start(fgain[:, :], A["final_gain"].rearrange("(a n) -> a n", a=1).partition_broadcast(P)).then_inc(small_in, 16)
                    act.dma_start(poolw[:, :, :], A["pool_w"][0].rearrange("g i o -> i g o")).then_inc(small_in, 16)
                    act.dma_start(up[0:LORA, :], A["w_lora_up"][0]).then_inc(small_in, 16)
                    act.dma_start(up[LORA:P, :], A["a_lora_up"][0]).then_inc(small_in, 16)
                    act.dma_start(w1[:, :, :], w_in_v[:, :, 0:POOL_COLS]).then_inc(w_in1, 16)
                    act.dma_start(wo1[:, :, :], w_out_v[:, 0:PT, :]).then_inc(w_in1, 16)
                    nc.scalar.preload_act_table_set("natural_log_exp_and_others")
                    act.wait_ge(vec_ok, 1)
                    nc.scalar.activation(sc[:, 0, :], v("c", 0, 8), ACT.Exp, scale=-1.0).then_inc(sc_exp, 1)

                @block.gpsimd
                def _(pool):
                    n = [0]

                    def link(ins):
                        n[0] += 1
                        ins.then_inc(pool_link, 1)
                        pool.wait_ge(pool_link, n[0])

                    def band(t, pattern, base, mult, op, fill):
                        link(nc.gpsimd.affine_select(out=t, in_=t, compare_op=op, fill=fill, base=base,
                                                     pattern=pattern, channel_multiplier=mult))

                    link(nc.gpsimd.memset(ident[:, :], 0.0))
                    band(ident[:, :], [[-1, P]], 0, 1, ALU.not_equal, 1.0)
                    link(nc.gpsimd.memset(ones[:, :], 1.0))
                    link(nc.gpsimd.memset(ident64[:, :], 0.0))
                    band(ident64[:, :], [[-1, HD]], 0, 1, ALU.not_equal, 1.0)
                    band(ident64[:, :], [[-1, HD]], -HD, 1, ALU.not_equal, 1.0)
                    link(nc.gpsimd.memset(head_sum[:, :], 0.0))
                    link(nc.gpsimd.memset(head_sum[0:HD, 0:HD], 1.0))
                    link(nc.gpsimd.memset(head_sum[HD:P, HD:P], 1.0))
                    link(nc.gpsimd.tensor_scalar(head_mean[:, :], head_sum[:, :], 1.0 / HD, None, ALU.mult))
                    link(nc.gpsimd.tensor_tensor(center[:, :], ident[:, :], head_mean[:, :], ALU.subtract))
                    link(nc.gpsimd.memset(gram_mask[:, :], 1.0))
                    for e in range(2):
                        g = gram_mask[half(e), :]
                        band(g[:, 0:HD], [[1, HD]], 0, -1, ALU.is_gt, 0.0)
                        band(g[:, HD:P], [[1, HD]], 0, -1, ALU.is_ge, 0.0)
                    link(nc.gpsimd.memset(diag16[:, :], 1.0))
                    for e in range(2):
                        d = diag16[half(e), :].rearrange("p (b j) -> p b j", j=16)
                        band(d, [[-16, 4], [0, 16]], 0, 1, ALU.is_ge, 0.0)
                        band(d, [[16, 4], [0, 16]], 15, -1, ALU.is_ge, 0.0)
                    link(nc.gpsimd.tensor_scalar(off16[:, :], diag16[:, :], -1.0, 1.0, ALU.mult, ALU.add))
                    link(nc.gpsimd.memset(restart[:, :], 1.0))
                    link(nc.gpsimd.memset(restart[:, :].rearrange("p (c t) -> p c t", t=C)[:, :, 0:1], 0.0))
                    for j, e in enumerate((EPS, KK_EPS, GN_EPS)):
                        link(nc.gpsimd.memset(eps[:, j:j + 1], e))
                    nc.gpsimd.memset(eps[:, 0:1], EPS).then_inc(consts, 1)

                @block.tensor
                def _(pe):
                    pe.wait_ge(rows_in, 16 * len(ROWS))
                    pe.wait_ge(consts, 1)
                    nc.tensor.transpose(bank[0][:, 0:NROWS], rows[0:NROWS, :], ident[0:NROWS, 0:NROWS]).then_inc(vec_ps, 1)
                    pe.wait_ge(sc_ok, 1)
                    for j in range(24):
                        pe.wait_ge(staged[j % 3], 16 * (j // 3 + 1))
                        for k in range(KT):
                            col = sc[:, 2, k:k + 1]
                            if j < 16:
                                last = nc.tensor.matmul(bank[1][:, j:j + 1], stage[:, j % 3, k], col,
                                                        start=(k == 0), stop=(k == KT - 1))
                            else:
                                g = j - 16
                                last = nc.tensor.matmul(bank[2 + g // 4][:, (g % 4) * P:(g % 4 + 1) * P],
                                                        col.broadcast_to([P, P]), stage[:, j % 3, k],
                                                        start=(k == 0), stop=(k == KT - 1))
                        last.then_inc(used, 1)

                @block.vector
                def _(dve):
                    n = [0]

                    def link(ins):
                        n[0] += 1
                        ins.then_inc(dve_link, 1)
                        dve.wait_ge(dve_link, n[0])

                    dve.wait_ge(vec_ps, 1)
                    nc.vector.tensor_copy(vec[:, :], bank[0][:, 0:NROWS]).then_inc(vec_ok, 1)
                    dve.wait_ge(vec_ok, 1)
                    dve.wait_ge(consts, 1)
                    dve.wait_ge(sc_exp, 1)
                    link(nc.vector.tensor_scalar_add(sc[:, 0, :], sc[:, 0, :], 1.0))
                    link(nc.vector.reciprocal(sc[:, 1, :], sc[:, 0, :]))
                    nc.vector.tensor_tensor(sc[:, 2, :], sc[:, 1, :], v("c", 0, 8), ALU.mult).then_inc(sc_ok, 1)
                    link(nc.vector.tensor_scalar(omu[:, :], v("mu", 0, MIX), -1.0, 1.0, ALU.mult, ALU.add))
                    link(nc.vector.tensor_scalar(negv[:, 0, :], v("w0", 0, NP), -1.0, None, ALU.mult))
                    link(nc.vector.tensor_scalar(negv[:, 1, :], v("a0", 0, NP), -1.0, None, ALU.mult))
                    link(nc.vector.tensor_scalar(oka[:, :], v("k_a", 0, NP), -1.0, 1.0, ALU.mult, ALU.add))
                    for p in range(NP):
                        link(nc.vector.tensor_scalar(rk_sum[:, p], head_sum[:, :], v("r_k", p), None, ALU.mult))
                    dve.wait_ge(used, 16)
                    nc.vector.tensor_tensor(mod[:, :], bank[1][:, 0:16], v("b_ada", 0, 16), ALU.add).then_inc(mod_ok, 1)
                    dve.wait_ge(mod_ok, 1)
                    link(nc.vector.tensor_scalar_add(gsc[:, :], mod[:, 8:16], 1.0))
                    link(nc.vector.tensor_tensor(gsc[:, :], gsc[:, :], v("norm_gain", 0, KT), ALU.mult))
                    dve.wait_ge(used, 24)
                    dve.wait_ge(small_in, 80)
                    for h in range(2):
                        link(nc.vector.tensor_tensor(gate_row[:, h * 512:(h + 1) * 512], bank[2 + h][:, :],
                                                     bgate[:, h * 512:(h + 1) * 512], ALU.add))
                    dve.wait_ge(w_in1, 32)
                    for k in range(PT):
                        link(nc.vector.scalar_tensor_tensor(out=wo1[:, k, :], in0=wo1[:, k, :], scalar=v("pool_scale", k),
                                                            in1=gate_row[:, :], op0=ALU.mult, op1=ALU.mult))

        with pass1 as st:
            x_in = sb("x_in", [P, 2, D], stack=st)
            xr = sb("xr", [P, 2, D], stack=st)
            junk = sb("junk", [P, D], BF16, stack=st)
            stat = sb("stat", [P, 3, 2], stack=st)
            xT = sb("xT", [P, KT, T1], stack=st)
            u = sb("u", [P, PT, HALO + T1], stack=st)
            gate = sb("gate", [P, PT, T1], stack=st)
            win_a = sb("win_a", [P, PT, HALO + T1], stack=st)
            win_b = sb("win_b", [P, PT, HALO + T1], stack=st)
            diff = sb("diff", [P, PT, T1], stack=st)
            yc = sb("yc", [P, PT, T1], stack=st)
            inv_cnt = sb("inv_cnt", [P, PT, 16], stack=st)

            x_loaded = sem("x_loaded", st)
            xr_loaded = [sem(f"xr_loaded{j}", st) for j in range(2)]
            h_stored = [sem(f"h_stored{j}", st) for j in range(2)]
            cnt_ready = sem("cnt_ready", st)
            norm_own = Signal(sem("norm_own", st), 5)
            halo_ready = Signal(sem("halo_ready", st), 1)
            gclamp_ready = Signal(sem("gclamp1_ready", st), 1)
            gln_own = Signal(sem("gln1_own", st), 1)
            gsig_ready = Signal(sem("gsig1_ready", st), 1)
            diff_first = Signal(sem("diff_first", st), 2 * PT)
            win_own = Signal(sem("win_own", st), 0)
            xn_ready = Signal(sem("xn_ready", st), 1)
            xT_ps = Signal(sem("xT_ps", st), 4)
            xT_ready = Signal(sem("xT_ready", st), KT)
            proj_ps = Signal(sem("proj_ps", st), 4)
            u_ready = Signal(sem("u_ready", st), PT)
            gx_ready = Signal(sem("gx_ready", st), PT)
            gate_ready = Signal(sem("gate_ready", st), 2)
            win_ready = Signal(sem("win_ready", st), PT)
            diff_ready = Signal(sem("diff_ready", st), PT)
            pool_ps = Signal(sem("pool_ps", st), 2)
            yc_ready = Signal(sem("yc_ready", st), 2)
            out_ps = Signal(sem("out_ps", st), 4)
            h_ready = Signal(sem("h_ready", st), 4)

            x_v = A["x"][0].rearrange("(n j p) d -> n p j d", p=P, j=2)
            x_t = A["x"][0].rearrange("(m p) d -> m p d", p=P)
            h1_t = h1.rearrange("(m p) d -> m p d", p=P)
            win = [win_a, win_b, win_a, win_b]

            with nc.Block() as block:
                @block.sync
                def _(sp):
                    def load_x(n):
                        let_through(sp, sp_gate)
                        sp.dma_start(x_in[:, :, :], rows_of(x_v, n)).then_inc(x_loaded, 16)

                    def load_residual(n):
                        let_through(sp, sp_gate)
                        for j in range(2):
                            sp.dma_start(xr[:, j], rows_of(x_t, 2 * n + j)).then_inc(xr_loaded[j], 16)

                    def store(n):
                        for j in range(2):
                            sp.wait_ge(h_ready.sem, h_ready.at(n, 2 * j + 2))
                            let_through(sp, sp_gate)
                            sp.dma_start(rows_of(h1_t, 2 * n + j), xr[:, j]).then_inc(h_stored[j], 16)

                    def step(n, more):
                        if more:
                            sp.wait_ge(xT_ps.sem, xT_ps.at(n, 4))
                            load_x(n + 1)
                        store(n - 1)
                        for j in range(2):
                            sp.wait_ge(h_stored[j], n * 16)
                        load_residual(n)

                    load_x(0)
                    load_residual(0)
                    sp.wait_ge(xT_ps.sem, xT_ps.at(0, 4))
                    load_x(1)
                    with sp.Fori(1, N1 - 1) as n:
                        step(n, True)
                    step(N1 - 1, False)
                    store(N1 - 1)
                    for j in range(2):
                        sp.wait_ge(h_stored[j], 16 * N1)

                @block.tensor
                def _(pe):
                    s = Steps(pe, None)

                    def transposes(n, first=False):
                        s.block(n)
                        s.wait(xn_ready, 1)
                        if not first:
                            s.wait(gx_ready, PT, back=1)
                            s.wait(gate_ready, 2, back=1)
                        for b in range(4):
                            for q in range(4):
                                k, j = 2 * b + q // 2, q % 2
                                last = nc.tensor.transpose(bank[b][:, q * P:(q + 1) * P], x_in[:, j, k * P:(k + 1) * P], ident[:, :])
                            last.then_inc(xT_ps.sem, 1)

                    def project(n, part):
                        s.block(n)
                        if part == 0:
                            s.wait(xT_ready, KT)
                        for t in range(part * PT, (part + 1) * PT):
                            for k in range(KT):
                                last = nc.tensor.matmul(bank[t // 2][:, (t % 2) * T1:(t % 2 + 1) * T1], w1[:, k, t * P:(t + 1) * P],
                                                        xT[:, k, :], start=(k == 0), stop=(k == KT - 1))
                            if t % 2:
                                last.then_inc(proj_ps.sem, 1)

                    def mix_groups(n, first=False):
                        s.block(n)
                        s.wait(diff_ready, PT)
                        if not first:
                            s.wait(yc_ready, 2, back=1)
                        for g in range(PT):
                            last = nc.tensor.matmul(bank[4 + g // 2][:, (g % 2) * T1:(g % 2 + 1) * T1], poolw[:, g, :],
                                                    diff[:, g, :], start=True, stop=True)
                            if g % 2:
                                last.then_inc(pool_ps.sem, 1)

                    def project_out(n, j, halves=(0, 1), first=False):
                        s.block(n)
                        s.wait(yc_ready, 2)
                        for h in halves:
                            if j:
                                s.wait(h_ready, h + 1)
                            elif not first:
                                s.wait(h_ready, 3 + h, back=1)
                            for k in range(PT):
                                last = nc.tensor.matmul(bank[6 + h][:, :], yc[:, k, j * P:(j + 1) * P],
                                                        wo1[:, k, h * 512:(h + 1) * 512], start=(k == 0), stop=(k == PT - 1))
                            last.then_inc(out_ps.sem, 1)

                    def run(n, first=False, more=True):
                        project(n, 0)
                        mix_groups(n - 1, first)
                        project(n, 1)
                        project_out(n - 1, 0, first=first)
                        project_out(n - 1, 1, halves=(0,))
                        if more:
                            transposes(n + 1)
                        project_out(n - 1, 1, halves=(1,))

                    transposes(0, first=True)
                    project(0, 0)
                    project(0, 1)
                    transposes(1)
                    run(1, first=True)
                    with pe.Fori(2, N1 - 1) as n:
                        run(n)
                    run(N1 - 1, more=False)
                    mix_groups(N1 - 1)
                    for j in range(2):
                        project_out(N1 - 1, j)

                @block.scalar
                def _(act):
                    s = Steps(act, norm_own)
                    nc.scalar.preload_act_table_set("natural_log_exp_and_others")

                    def norm(n, first=False):
                        s.block(n)
                        act.wait_ge(x_loaded, n * 16 + 16)
                        for j in range(2):
                            s(nc.scalar.activation(junk[:, :], x_in[:, j, :], ACT.Square, accum_out=stat[:, 0, j:j + 1]))
                        s(nc.scalar.activation(stat[:, 1, :], stat[:, 0, :], ACT.Ln, scale=1.0 / D, bias=eps[:, 0:1]))
                        s(nc.scalar.activation(stat[:, 2, :], stat[:, 1, :], ACT.Exp, scale=-0.5))
                        s(nc.scalar.activation(x_in[:, 0, :], x_in[:, 0, :], ACT.Copy, scale=stat[:, 2, 0:1]))
                        s(nc.scalar.activation(x_in[:, 1, :], x_in[:, 1, :], ACT.Copy, scale=stat[:, 2, 1:2]), xn_ready)
                        for b in range(4):
                            s.wait(xT_ps, b + 1)
                            for q in range(2):
                                k = 2 * b + q
                                s(nc.scalar.activation(xT[:, k, :], bank[b][:, q * T1:(q + 1) * T1], ACT.Identity,
                                                       scale=gsc[:, k:k + 1], bias=mod[:, k:k + 1]), xT_ready, hold=False)

                    def evacuate(n, first=False):
                        s.block(n)
                        if first:
                            s(nc.scalar.activation(u[:, :, 0:HALO], ident[:, 0:PT * HALO].rearrange("p (g h) -> p g h", g=PT),
                                                   ACT.Copy, scale=0.0), halo_ready)
                        else:
                            s.wait(diff_ready, PT, back=1)
                            s(nc.scalar.activation(u[:, :, 0:HALO], u[:, :, T1:T1 + HALO], ACT.Copy), halo_ready)
                        for g in range(PT):
                            s.wait(proj_ps, g // 2 + 1)
                            s(nc.scalar.activation(u[:, g, HALO:], bank[g // 2][:, (g % 2) * T1:(g % 2 + 1) * T1], ACT.Copy), u_ready)
                        if not first:
                            s.wait(yc_ready, 2, back=1)
                        for g in range(PT):
                            s.wait(proj_ps, g // 2 + 3)
                            s(nc.scalar.activation(gate[:, g, :], bank[2 + g // 2][:, (g % 2) * T1:(g % 2 + 1) * T1], ACT.Exp,
                                                   scale=-1.0), gx_ready)

                    def sigmoid(n):
                        s.block(n)
                        s.wait(gclamp_ready, 1)
                        s(nc.scalar.activation(gate[:, :, :], gate[:, :, :], ACT.Ln, bias=1.0), gln_own)
                        s(nc.scalar.activation(gate[:, :, :], gate[:, :, :], ACT.Exp, scale=-1.0), gsig_ready)

                    norm(0, first=True)
                    evacuate(0, first=True)
                    sigmoid(0)
                    norm(1)
                    with act.Fori(1, N1 - 1) as n:
                        evacuate(n)
                        sigmoid(n)
                        norm(n + 1)
                    evacuate(N1 - 1)
                    sigmoid(N1 - 1)

                @block.gpsimd
                def _(pool):
                    for k in range(KT):
                        pool.dma_start(w2[:, k], w_in_v[:, k, POOL_COLS:]).then_inc(w2_loaded, 16)
                    pool.dma_start(wo2[:, :, :], w_out_v[:, PT:, :]).then_inc(w2_loaded, 16)
                    s = Steps(pool, win_own)
                    for g, w in enumerate(WIN):
                        for t in range(16):
                            last = nc.gpsimd.memset(inv_cnt[:, g, t:t + 1], 1.0 / min(t + 1, w))
                    last.then_inc(cnt_ready, 1)

                    def windows(n, first=False):
                        s.block(n)
                        if not first:
                            s.wait(diff_ready, PT, back=1)
                        s.wait(u_ready, PT)
                        src = u
                        for g in range(PT):
                            w = WIN[g]
                            s(nc.gpsimd.tensor_tensor(win[g][:, g:, w - 1:], src[:, g:, w - 1:], src[:, g:, w - 1 - w // 2:HALO + T1 - w // 2],
                                                      ALU.add), win_ready)
                            src = win[g]

                    windows(0, first=True)
                    with pool.Fori(1, N1) as n:
                        windows(n)

                @block.vector
                def _(dve):
                    s = Steps(dve, None)
                    dve.wait_ge(cnt_ready, 1)

                    def clamp(n):
                        s.block(n)
                        s.wait(gx_ready, PT)
                        s(nc.vector.tensor_scalar(gate[:, :, :], gate[:, :, :], LN_MAX, None, ALU.min), gclamp_ready)

                    def gates(n):
                        s.block(n)
                        s.wait(gsig_ready, 1)
                        for b in range(2):
                            g = gate[:, 2 * b:2 * b + 2, :].rearrange("p g t -> p (g t)")
                            s(nc.vector.tensor_tensor(g, bank[2 + b][:, :], g, ALU.mult), gate_ready)

                    def differences(n, first=False):
                        s.block(n)
                        if not first:
                            s.wait(pool_ps, 2, back=1)
                        lo = 16 if first else 0
                        for g in range(PT):
                            s.wait(win_ready, g + 1)
                            if first:
                                s(nc.vector.tensor_tensor(diff[:, g, 0:16], win[g][:, g, HALO:HALO + 16], inv_cnt[:, g, :], ALU.mult), diff_first)
                                s(nc.vector.tensor_tensor(diff[:, g, 0:16], diff[:, g, 0:16], u[:, g, HALO:HALO + 16], ALU.subtract), diff_first)
                            s(nc.vector.scalar_tensor_tensor(out=diff[:, g, lo:], in0=win[g][:, g, HALO + lo:], scalar=1.0 / WIN[g],
                                                             in1=u[:, g, HALO + lo:], op0=ALU.mult, op1=ALU.subtract), diff_ready)

                    def mixed(n):
                        s.block(n)
                        for b in range(2):
                            s.wait(pool_ps, b + 1)
                            s(nc.vector.tensor_tensor(yc[:, 2 * b:2 * b + 2, :].rearrange("p g t -> p (g t)"), bank[4 + b][:, :],
                                                      gate[:, 2 * b:2 * b + 2, :].rearrange("p g t -> p (g t)"), ALU.mult), yc_ready)

                    def residual(n, j):
                        s.block(n)
                        s.count[h_ready] = 2 * j
                        dve.wait_ge(xr_loaded[j], n * 16 + 16)
                        for h in range(2):
                            s.wait(out_ps, 2 * j + h + 1)
                            s(nc.vector.tensor_tensor(xr[:, j, h * 512:(h + 1) * 512], bank[6 + h][:, :],
                                                      xr[:, j, h * 512:(h + 1) * 512], ALU.add), h_ready)

                    clamp(0)
                    gates(0)
                    differences(0, first=True)
                    with dve.Fori(1, N1) as n:
                        mixed(n - 1)
                        clamp(n)
                        residual(n - 1, 0)
                        gates(n)
                        residual(n - 1, 1)
                        differences(n)
                    mixed(N1 - 1)
                    for j in range(2):
                        residual(N1 - 1, j)

        with ExitStack() as st:
            def new(name, shape, dt=F32):
                return sb(name, shape, dt, stack=st)

            def signal(name, per, start=0):
                return Signal(sem(name, st), per, start)

            x_in = new("x2_in", [P, D])
            hr = gate_row
            junk = new("junk2", [P, D], BF16)
            stat = new("stat2", [P, 3])
            hstat = new("hstat", [P, 3])
            xT = new("xT2", [P, KT, T2])
            mix = new("mix", [P, MIX, T2])
            prev = new("prev", [P, MIX, 1 + T2])
            rg = new("rg", [P, NP, T2])
            rgate = new("rgate", [P, NP, T2])
            th = new("th", [P, T2])
            sig = new("sig", [P, 2, NP, T2])
            G = new("G", [P, NP, T2])
            egx = new("egx", [P, NP, T2])
            egi = new("egi", [P, NP, T2])
            kk = new("kk", [P, NP, T2])
            rn = new("rn", [P, NP, T2])
            t2 = new("t2", [P, NP, T2])
            k2 = new("k2", [P, NP, T2])
            rk = new("rk", [P, NP, T2])
            bonus = new("bonus", [P, NP, T2])
            LA = [new(f"LA{e}", [P, NP, NC, 2, C]) for e in range(2)]
            BK = new("BK", [P, NP, NC, 2, C])
            SM = [[new(f"SM{j}{e}", [P, NP, 2, C]) for e in range(2)] for j in range(NC)]
            SV = [new(f"SV{e}", [P, NP, HD]) for e in range(2)]
            UV = [new(f"UV{e}", [P, NP, HD]) for e in range(2)]
            BT = [new(f"BT{e}", [P, NC, NP, HD]) for e in range(2)]
            DT = [new(f"DT{j}", [P, NP, P]) for j in range(NC)]
            ET = [new(f"ET{j}", [P, NP, P]) for j in range(NC)]
            Qx = [new(f"Qx{j}", [P, NP, P]) for j in range(NC)]
            Dx = [kk, t2]
            D2 = [k2, rk]
            Q1 = [new(f"Q1_{j}", [P, NP, HD]) for j in range(NC)]
            QD = [new(f"QD{j}", [P, NP, HD]) for j in range(NC)]
            Qr = [new(f"Qr{j}", [P, NP, HD]) for j in range(NC)]
            R = new("R", [P, NP, HD])
            Vt = new("Vt", [P, NC, NP, HD])
            Y = new("Y", [P, NP, T2])
            rs = new("rs", [P, NP, T2])
            stmp = new("stmp", [P, NP, HD])
            dend = new("dend", [P, NP, NC])

            x_loaded, h_loaded, stored = sem("x2_loaded", st), sem("h_loaded", st), sem("stored", st)
            wo2_ready, zero_ready, zero_link, set_link = (
                sem("wo2_ready", st), sem("zero_ready", st), sem("zero_link", st), sem("set_link", st))
            norm_own = signal("norm2_own", 3)
            head_act = signal("head_act", 1)
            head_dve = signal("head_dve", HEAD_DVE)
            head_pool = signal("head_pool", 1)
            dve_own = signal("dve2_own", DVE_OWN)
            pool_own = signal("pool2_own", 2 * NC)
            act_own = signal("act2_own", 1)
            act_half = signal("act_half", NC)
            tail_act = signal("tail_act", 1)
            tail_dve = signal("tail_dve", NP + 2)
            xn_ready = signal("xn2_ready", 1)
            xT_ps = signal("xT2_ps", 2)
            xT_ready = signal("xT2_ready", KT)
            group_ps = signal("group_ps", 5)
            rg_ready = signal("rg_ready", 1)
            mix_in = signal("mix_in", 2 * MIX)
            mix_ready = signal("mix_ready", 4)
            carry_ready = signal("carry_ready", 1)
            eth_ready = signal("eth_ready", 1)
            k2_ready = signal("k2_ready", 1)
            th_ready = signal("th_ready", 1)
            lora_ps = signal("lora_ps", 2)
            e_ready = signal("e_ready", 2 * NP)
            clamp_ready = signal("clamp_ready", 2)
            ln_own = signal("ln_own", 2)
            sig_ready = signal("sig_ready", 2)
            G_ready = signal("G_ready", 1)
            gprev_ready = signal("gprev_ready", 1)
            exps_ready = signal("exps_ready", 3)
            kk_ready = signal("kk_ready", 1)
            kk2_ready = signal("kk2_ready", 1)
            norm_ps = signal("norm_ps", 1)
            rn_ready = signal("rn_ready", 1)
            rk_ready = signal("rk_ready", 1)
            bonus_ps = signal("bonus_ps", 1)
            lhs_ready = signal("lhs_ready", 1)
            erg_ready = signal("erg_ready", 1)
            gclamp_ready = signal("gclamp_ready", 1)
            gln_own = signal("gln_own", 1)
            gsig_ready = signal("gsig_ready", 1)
            rgate_ready = signal("rgate_ready", 1)
            prep_ready = signal("prep_ready", 1)
            kt_ready = signal("kt_ready", 1)
            gram_ps = signal("gram_ps", 2 * NC)
            vt_ps = signal("vt_ps", 1)
            bt_ps = signal("bt_ps", 2)
            inv_ps = signal("inv_ps", INV * NC)
            r_ps = signal("r_ps", NC)
            u_ps = signal("u_ps", NC)
            s_ps = signal("s_ps", NC)
            y_ps = signal("y_ps", NC)
            sm_ready = signal("sm_ready", 2 * NC)
            dt_ready = signal("dt_ready", NC)
            q1_ready = signal("q1_ready", NC)
            horner_ready = signal("horner_ready", 6 * NC)
            qd_ready = signal("qd_ready", NC)
            g_ready = signal("g_ready", 2 * NC)
            q_ready = signal("q_ready", NC)
            r_ready = signal("r_ready", NC)
            s_ready = signal("s_ready", NC)
            v_ready = signal("v_ready", 1)
            bt_ready = signal("bt_ready", 2)
            d_ready = signal("d_ready", NC)
            d2_ready = signal("d2_ready", NC)
            td_ready = signal("td_ready", NC)
            gt_ready = signal("gt_ready", NC)
            u_ready = signal("u2_ready", NC)
            y_ready = signal("y_ready", NC)
            et_ready = signal("et_ready", NC)
            la_ready = signal("la_ready", NC)
            sv_ready = signal("sv_ready", 2)
            uv_ready = signal("uv_ready", 2)
            v1_ready = signal("v1_ready", 4)
            ysq_ready = signal("ysq_ready", 1)
            var_ps = signal("var_ps", 1)
            rs_ready = signal("rs_ready", 1)
            y2_ready = signal("y2_ready", 1)
            out_ps = signal("out2_ps", 2)
            h_ready = signal("h2_ready", 2)
            hn_ready = signal("hn_ready", 1)
            hn_own = signal("hn_own", 2)
            out_ready = signal("out_ready", 1)

            GROUPS = [(12, 1, 0), (0, 4, 1), (4, 4, 0), (13, 4, 1), (8, 4, 0)]
            MIX_GROUP = [0, 1, 2, 4]
            MIXED = [2, 10, 18, 26]
            SLOTS = [(gr, q, k) for gr, (_, n, _) in enumerate(GROUPS) for q in range(n) for k in (0, KT // 2)]

            x_t = A["x"][0].rearrange("(m p) d -> m p d", p=P)
            h1_t = h1.rearrange("(m p) d -> m p d", p=P)
            out_t = out[0].rearrange("(m p) d -> m p d", p=P)
            flat = "p a b -> p (a b)"

            def each_block(eng, run):
                run(0, True, 2)
                with eng.Fori(1, N2 - 2) as n:
                    run(n, False, 2)
                run(N2 - 2, False, 1)
                run(N2 - 1, False, 0)

            with nc.Block() as block:
                @block.sync
                def _(sp):
                    def load_x(n):
                        sp.wait_ge(xT_ps.sem, xT_ps.at(n - 1, 2))
                        let_through(sp, sp_gate)
                        sp.dma_start(x_in[:, :], rows_of(x_t, n)).then_inc(x_loaded, 16)

                    def store(n):
                        sp.wait_ge(out_ready.sem, out_ready.at(n, 1))
                        let_through(sp, sp_gate)
                        sp.dma_start(rows_of(out_t, n), hr[:, :]).then_inc(stored, 16)
                        sp.wait_ge(stored, n * 16 + 16)

                    def run(n, first, ahead):
                        if ahead == 2:
                            load_x(n + 2)
                        if not first:
                            store(n - 1)
                            let_through(sp, sp_gate)
                        sp.dma_start(hr[:, :], rows_of(h1_t, n)).then_inc(h_loaded, 16)

                    sp.dma_start(x_in[:, :], x_t[0]).then_inc(x_loaded, 16)
                    load_x(1)
                    sp.wait_ge(wo2_ready, 1)
                    each_block(sp, run)
                    store(N2 - 1)

                @block.tensor
                def _(pe):
                    s = Steps(pe, None)
                    nx = Steps(pe, None)
                    pv = Steps(pe, None)

                    pe.wait_ge(w2_loaded, 16 * (KT + 1))
                    pe.wait_ge(zero_ready, 1)

                    def transposes(b):
                        if b:
                            nx.wait(xT_ready, KT // 2)
                        for q in range(4):
                            k = 4 * b + q
                            last = nc.tensor.transpose(bank[0][:, q * P:(q + 1) * P], x_in[:, k * P:(k + 1) * P], ident[:, :])
                        last.then_inc(xT_ps.sem, 1)

                    def project(m, prologue=False):
                        gr, q, k0 = SLOTS[m]
                        t0, w, b = GROUPS[gr]
                        if q == 0 and k0 == 0:
                            if gr == 0:
                                nx.wait(xT_ready, KT)
                            elif gr > 1:
                                nx.wait(mix_in, MIXED[gr - 2])
                            elif not prologue:
                                s.wait(prep_ready, 1)
                        for k in range(k0, k0 + KT // 2):
                            last = nc.tensor.matmul(bank[b][:, q * P:(q + 1) * P], w2[:, k, (t0 + q) * P:(t0 + q + 1) * P], xT[:, k, :],
                                                    start=(k == 0), stop=(k == KT - 1))
                        if q == w - 1 and k0:
                            last.then_inc(group_ps.sem, 1)

                    def low_rank():
                        nx.wait(mix_ready, 1)
                        nx.wait(th_ready, 1)
                        for p in range(NP):
                            for i, (part, rhs) in enumerate(((slice(0, LORA), th[0:LORA, :]), (slice(LORA, P), mix[LORA:P, 12, :]))):
                                last = nc.tensor.matmul(bank[2 + i][:, p * P:(p + 1) * P], up[part, p * P:(p + 1) * P], rhs,
                                                        start=True, stop=True)
                                if p == NP - 1:
                                    last.then_inc(lora_ps.sem, 1)

                    def key_norm():
                        nx.wait(kk2_ready, 1)
                        nc.tensor.matmul(bank[4][:, :], head_sum[:, :], rn[:, :, :].rearrange(flat), start=True, stop=True)\
                            .then_inc(norm_ps.sem, 1)

                    def bonus_sum():
                        nx.wait(rk_ready, 1)
                        nx.wait(rg_ready, 1)
                        for p in range(NP):
                            last = nc.tensor.matmul(bank[1][:, p * P:(p + 1) * P], rk_sum[:, p], rk[:, p], start=True, stop=True)
                        last.then_inc(bonus_ps.sem, 1)

                    def variance():
                        pv.wait(ysq_ready, 1)
                        nc.tensor.matmul(bank[6][:, :], head_mean[:, :], rs[:, :, :].rearrange(flat), start=True, stop=True)\
                            .then_inc(var_ps.sem, 1)

                    def out_half(h):
                        pv.wait(y2_ready, 1)
                        for p in range(NP):
                            last = nc.tensor.matmul(bank[(4, 7)[h]][:, :], Y[:, p], wo2[:, p, h * 512:(h + 1) * 512],
                                                    start=(p == 0), stop=(p == NP - 1))
                        last.then_inc(out_ps.sem, 1)

                    def inverses(fill, other):
                        def full(j, lhsT, rhs):
                            for p in range(NP):
                                last = nc.tensor.matmul(bank[2 + j][:, p * P:(p + 1) * P], lhsT[:, p], rhs[:, p], start=True, stop=True)
                            last.then_inc(inv_ps.sem, 1)

                        def turn(j, t):
                            for p in range(NP):
                                last = nc.tensor.transpose(bank[2 + j][:, p * P:(p + 1) * P], t[:, p], ident[:, :])
                            last.then_inc(inv_ps.sem, 1)

                        def apply(j, i, lhsT, rhs):
                            o = (i % 2) * 256
                            nc.tensor.matmul(bank[2 + j][:, o:o + HD], lhsT[:, 0], rhs[:, 0], start=True, stop=True)
                            for p in range(1, NP):
                                for e in range(2):
                                    h = half(e)
                                    last = nc.tensor.matmul(bank[2 + j][h, o + p * HD:o + (p + 1) * HD], lhsT[h, p, h], rhs[h, p],
                                                            start=True, stop=True)
                            last.then_inc(inv_ps.sem, 1)

                        for j in range(NC):
                            s.wait(dt_ready, j + 1)
                            turn(j, DT[j])
                        for j in range(NC):
                            s.wait(d_ready, j + 1)
                            full(j, DT[j], Dx[j])
                        fill()
                        for i in range(7):
                            for j in range(NC):
                                if i:
                                    s.wait(horner_ready, NC * (i - 1) + j + 1)
                                else:
                                    s.wait(d2_ready, j + 1)
                                    s.wait(q1_ready, j + 1)
                                apply(j, i, D2[j], Qr[j] if i else Q1[j])
                            fill(2 if i in (1, 3, 5) else 1)
                            if i in (2, 4):
                                other(i // 2 - 1)
                        for j in range(NC):
                            s.wait(qd_ready, j + 1)
                            turn(j, Qx[j])
                        fill()
                        for j in range(NC):
                            s.wait(td_ready, j + 1)
                            s.wait(et_ready, j + 1)
                            full(j, ET[j], Dx[j])
                        fill()
                        for i in range(3):
                            for j in range(NC):
                                if i:
                                    s.wait(g_ready, NC * (i - 1) + j + 1)
                                else:
                                    s.wait(gt_ready, j + 1)
                                apply(j, i, D2[j], Qr[j] if i else QD[j])
                            fill()

                    def from_state(j):
                        s.wait(la_ready, j + 1)
                        if j:
                            s.wait(v1_ready, 2)
                            s.wait(s_ready, 1)
                        else:
                            s.wait(sv_ready, 2)
                            s.wait(bt_ready, 2)
                        for p in range(NP):
                            for e in range(2):
                                last = nc.tensor.matmul(bank[5][half(e), p * HD:(p + 1) * HD], LA[e][:, p, j, 0], SV[e][:, p],
                                                        start=True, stop=True)
                        last.then_inc(r_ps.sem, 1)

                    def solve(j):
                        s.wait(q_ready, j + 1)
                        s.wait(r_ready, j + 1)
                        for p in range(NP):
                            last = nc.tensor.matmul(bank[5][:, 256 + p * HD:256 + (p + 1) * HD], Qx[j][:, p], R[:, p], start=True, stop=True)
                        last.then_inc(u_ps.sem, 1)

                    def state_and_output(j, first=False):
                        if j:
                            s.wait(v1_ready, 4)
                        else:
                            s.wait(uv_ready, 2)
                            if not first:
                                pv.wait(h_ready, 2)
                        s.wait(u_ready, j + 1)
                        for p in range(NP):
                            for e in range(2):
                                last = nc.tensor.matmul(bank[7][half(e), p * HD:(p + 1) * HD], BT[e][:, j, p], UV[e][:, p],
                                                        start=True, stop=True)
                        last.then_inc(s_ps.sem, 1)
                        if j:
                            s.wait(y_ready, j)
                        for p in range(NP):
                            for e in range(2):
                                o = bank[6][half(e), p * HD:(p + 1) * HD]
                                nc.tensor.matmul(o, UV[e][:, p], SM[j][e][:, p, 1], start=True, stop=False)
                                last = nc.tensor.matmul(o, SV[e][:, p], LA[e][:, p, j, 1], start=False, stop=True)
                        last.then_inc(y_ps.sem, 1)

                    def run(n, first, ahead):
                        s.block(n)
                        if not first:
                            pv.block(n - 1)
                        nx.block(n + 1)
                        m = [0]

                        def fill(k=1):
                            for _ in range(k):
                                if ahead and m[0] < len(SLOTS):
                                    project(m[0])
                                    m[0] += 1

                        if first:
                            pe.wait_ge(wo2_ready, 1)
                        else:
                            variance()
                            pv.wait(s_ready, NC)
                        s.wait(kt_ready, 1)
                        s.wait(lhs_ready, 1)
                        for j in range(NC):
                            for p in range(NP):
                                for e in range(2):
                                    last = nc.tensor.matmul(bank[((2, 3), (4, 7))[j][e]][:, p * P:(p + 1) * P], BK[half(e), p, j].rearrange(flat),
                                                            LA[e][half(e), p, j].rearrange(flat), start=True, stop=True)
                                    if p == NP - 1:
                                        last.then_inc(gram_ps.sem, 1)
                        if ahead:
                            nx.wait(xn_ready, 1)
                            s.wait(mix_in, MIXED[3])
                            transposes(0)
                        s.wait(mix_ready, 4)
                        if not first:
                            pv.wait(rs_ready, 1)
                        for j in range(NC):
                            for p in range(NP):
                                for e in range(2):
                                    o = j * 256 + p * HD
                                    last = nc.tensor.matmul(bank[5][half(1 - e), o:o + HD], mix[:, 8 + p, j * C:(j + 1) * C],
                                                            center[:, half(e)], start=True, stop=True)
                        last.then_inc(vt_ps.sem, 1)
                        for e in range(2):
                            if e:
                                s.wait(v_ready, 1)
                                if ahead:
                                    transposes(1)
                            for j in range(NC):
                                for p in range(NP):
                                    o = j * 256 + p * HD
                                    last = nc.tensor.transpose(bank[(6, 5)[e]][:, o:o + HD], BK[half(e), p, j].rearrange(flat),
                                                               ident[half(e), half(e)])
                            last.then_inc(bt_ps.sem, 1)
                        fill(2)
                        inverses(fill, (lambda h: None) if first else out_half)
                        while ahead and m[0] < 18:
                            fill()
                        from_state(0)
                        if ahead:
                            s.wait(q_ready, NC)
                            low_rank()
                        solve(0)
                        fill(2)
                        state_and_output(0, first)
                        fill(2)
                        if ahead:
                            key_norm()
                        from_state(1)
                        fill(2)
                        solve(1)
                        fill(2)
                        state_and_output(1)
                        if ahead:
                            bonus_sum()
                        fill(len(SLOTS))

                    nx.block(0)
                    nx.wait(xn_ready, 1)
                    transposes(0)
                    transposes(1)
                    for m in range(len(SLOTS)):
                        project(m, prologue=True)
                    low_rank()
                    key_norm()
                    bonus_sum()
                    each_block(pe, run)
                    pv.block(N2 - 1)
                    variance()
                    out_half(0)
                    out_half(1)

                @block.scalar
                def _(act):
                    s = Steps(act, act_own)
                    hd = Steps(act, head_act)
                    nx = Steps(act, norm_own)
                    pv = Steps(act, tail_act)

                    def norm(n):
                        nx.block(n)
                        act.wait_ge(x_loaded, n * 16 + 16)
                        nx(nc.scalar.activation(junk[:, :], x_in[:, :], ACT.Square, accum_out=stat[:, 0:1]))
                        nx(nc.scalar.activation(stat[:, 1:2], stat[:, 0:1], ACT.Ln, scale=1.0 / D, bias=eps[:, 0:1]))
                        nx(nc.scalar.activation(stat[:, 2:3], stat[:, 1:2], ACT.Exp, scale=-0.5))
                        nx(nc.scalar.activation(x_in[:, :], x_in[:, :], ACT.Copy, scale=stat[:, 2:3]), xn_ready)

                    def take_xT(n, b):
                        nx.block(n)
                        nx.count[xT_ready] = 4 * b
                        nx.wait(xT_ps, b + 1)
                        for q in range(4):
                            k = 4 * b + q
                            nx(nc.scalar.activation(xT[:, k], bank[0][:, q * P:(q + 1) * P], ACT.Identity, scale=gsc[:, k:k + 1],
                                                    bias=mod[:, k:k + 1]), xT_ready, hold=False)

                    def take_group(n, gr):
                        nx.block(n)
                        t0, w, b = GROUPS[gr]
                        nx.wait(group_ps, gr + 1)
                        if gr == 3:
                            nx(nc.scalar.activation(rg[:, :, :].rearrange(flat), bank[b][:, :], ACT.Copy), rg_ready, hold=False)
                            return
                        for q in range(w):
                            src = bank[b][:, q * P:(q + 1) * P]
                            t = t0 + q
                            nx(nc.scalar.activation(mix[:, t], src, ACT.Copy, scale=omu[:, t:t + 1]), mix_in, hold=False)
                            nx(nc.scalar.activation(prev[:, t, 1:], src, ACT.Copy, scale=v("mu", t)), mix_in, hold=False)

                    def exp_tanh():
                        hd.wait(mix_ready, 1)
                        hd(nc.scalar.activation(th[0:LORA, :], mix[0:LORA, 12, :], ACT.Exp, scale=-2.0), eth_ready)

                    def exp_low_rank(i):
                        hd.wait(lora_ps, i + 1)
                        for p in range(NP):
                            hd(nc.scalar.activation(sig[:, i, p], bank[2 + i][:, p * P:(p + 1) * P], ACT.Exp, scale=-1.0,
                                                    bias=negv[:, i, p:p + 1]), e_ready, hold=False)

                    def sigmoid(i):
                        hd.wait(clamp_ready, i + 1)
                        hd(nc.scalar.activation(sig[:, i], sig[:, i], ACT.Ln, bias=1.0), ln_own)
                        hd(nc.scalar.activation(sig[:, i], sig[:, i], ACT.Exp, scale=-1.0), sig_ready)

                    def key_scale():
                        hd.wait(norm_ps, 1)
                        hd(nc.scalar.activation(rn[:, :, :].rearrange(flat), bank[4][:, :], ACT.Ln, bias=eps[:, 1:2]))
                        hd(nc.scalar.activation(rn[:, :, :], rn[:, :, :], ACT.Exp, scale=-0.5), rn_ready)

                    def decays():
                        hd.wait(G_ready, 1)
                        hd(nc.scalar.activation(egi[:, :, :], G[:, :, :], ACT.Exp, scale=DECAY), exps_ready)
                        hd.wait(gprev_ready, 1)
                        hd(nc.scalar.activation(sig[:, 0], G[:, :, :], ACT.Exp, scale=-DECAY), exps_ready)
                        hd(nc.scalar.activation(egx[:, :, :], egx[:, :, :], ACT.Exp, scale=-DECAY), exps_ready)

                    def group_scale():
                        pv.wait(var_ps, 1)
                        pv(nc.scalar.activation(rs[:, :, :].rearrange(flat), bank[6][:, :], ACT.Ln, bias=eps[:, 2:3]))
                        pv(nc.scalar.activation(rs[:, :, :], rs[:, :, :], ACT.Exp, scale=-0.5), rs_ready)

                    def residual_norm(n):
                        fn = Steps(act, hn_own)
                        fn.block(n)
                        fn.wait(h_ready, 2)
                        fn(nc.scalar.activation(junk[:, :], hr[:, :], ACT.Square, accum_out=hstat[:, 0:1]))
                        fn(nc.scalar.activation(hstat[:, 1:2], hstat[:, 0:1], ACT.Ln, scale=1.0 / D, bias=eps[:, 0:1]))
                        fn(nc.scalar.activation(hstat[:, 2:3], hstat[:, 1:2], ACT.Exp, scale=-0.5), hn_ready)

                    def take_u(j):
                        s.wait(u_ps, j + 1)
                        if j:
                            s.wait(y_ps, j)
                        s(nc.scalar.activation(UV[0][half(0), :, :].rearrange(flat), bank[5][half(0), 256:512], ACT.Copy), act_half, hold=False)
                        s(nc.scalar.activation(UV[1][half(1), :, :].rearrange(flat), bank[5][half(1), 256:512], ACT.Copy), u_ready)

                    def take_y(j):
                        s.wait(y_ps, j + 1)
                        s(nc.scalar.activation(Y[:, :, j * C:(j + 1) * C], bank[6][:, 0:256].rearrange("p (a b) -> p a b", b=C),
                                               ACT.Copy), y_ready)

                    def run(n, first, ahead):
                        s.block(n)
                        hd.block(n + 1)
                        if not first:
                            pv.block(n - 1)
                            group_scale()
                        if ahead:
                            take_xT(n + 1, 0)
                        s.wait(vt_ps, 1)
                        s(nc.scalar.activation(Vt[:, :, :, :].rearrange("p j a b -> p (j a b)"), bank[5][:, :], ACT.Copy), v_ready)
                        if ahead:
                            take_xT(n + 1, 1)
                        for b in range(2):
                            s.wait(bt_ps, b + 1)
                            s(nc.scalar.activation(BT[b][:, :, :, :].rearrange("p j a b -> p (j a b)"), bank[(6, 5)[b]][:, :], ACT.Copy), bt_ready)
                        for j in range(NC):
                            s.wait(inv_ps, j + 1)
                            s(nc.scalar.activation(Dx[j][:, :, :].rearrange(flat), bank[2 + j][:, :], ACT.Copy), d_ready)
                        for j in range(NC):
                            s.wait(inv_ps, NC + j + 1)
                            s(nc.scalar.activation(D2[j][:, :, :].rearrange(flat), bank[2 + j][:, :], ACT.Copy), d2_ready)
                        if ahead:
                            s.wait(carry_ready, 1)
                            take_group(n + 1, 0)
                            exp_tanh()
                        if not first:
                            pv.wait(y2_ready, 1)
                        s(nc.scalar.activation(rgate[:, :, :], rg[:, :, :], ACT.Exp, scale=-1.0), erg_ready)
                        if ahead:
                            take_group(n + 1, 1)
                        s.wait(gclamp_ready, 1)
                        s(nc.scalar.activation(rgate[:, :, :], rgate[:, :, :], ACT.Ln, bias=1.0), gln_own)
                        s(nc.scalar.activation(rgate[:, :, :], rgate[:, :, :], ACT.Exp, scale=-1.0), gsig_ready)
                        for j in range(NC):
                            s.wait(inv_ps, NC * 9 + j + 1)
                            s(nc.scalar.activation(Dx[j][:, :, :].rearrange(flat), bank[2 + j][:, :], ACT.Copy), td_ready)
                        for j in range(NC):
                            s.wait(inv_ps, NC * 10 + j + 1)
                            s(nc.scalar.activation(D2[j][:, :, :].rearrange(flat), bank[2 + j][:, :], ACT.Copy), gt_ready)
                        if not first:
                            residual_norm(n - 1)
                        if ahead:
                            take_group(n + 1, 2)
                        if ahead == 2:
                            norm(n + 2)
                        if ahead:
                            exp_low_rank(0)
                        take_u(0)
                        if ahead:
                            exp_low_rank(1)
                        s.wait(y_ps, 1)
                        for i, t in enumerate((SV, UV)):
                            for e in range(2):
                                o = half(1 - e)
                                s(nc.scalar.activation(t[e][o], Vt[o, 1], ACT.Copy), v1_ready, hold=False)
                        if not first:
                            pv.wait(out_ps, 2)
                        take_y(0)
                        if ahead:
                            sigmoid(0)
                            key_scale()
                            sigmoid(1)
                        take_u(1)
                        if ahead:
                            decays()
                            s.wait(rgate_ready, 1)
                            take_group(n + 1, 3)
                        take_y(1)
                        s(nc.scalar.activation(rs[:, :, :], Y[:, :, :], ACT.Square), ysq_ready)
                        if ahead:
                            take_group(n + 1, 4)
                            hd.end("act head")
                        s.end("act")

                    nc.scalar.preload_act_table_set("natural_log_exp_and_others")
                    act.wait_ge(zero_ready, 1)
                    norm(0)
                    take_xT(0, 0)
                    take_xT(0, 1)
                    hd.block(0)
                    take_group(0, 0)
                    exp_tanh()
                    for gr in range(1, 5):
                        take_group(0, gr)
                    norm(1)
                    exp_low_rank(0)
                    exp_low_rank(1)
                    sigmoid(0)
                    key_scale()
                    sigmoid(1)
                    decays()
                    each_block(act, run)
                    pv.block(N2 - 1)
                    group_scale()
                    residual_norm(N2 - 1)

                @block.gpsimd
                def _(pool):
                    s = Steps(pool, pool_own)
                    hd = Steps(pool, head_pool)

                    def copy(to, of, one):
                        return nc.gpsimd.tensor_tensor(to, of, one, ALU.mult)

                    def ones_of(part):
                        return ones[part, :].unsqueeze(1).broadcast_to([HD, NP, HD])

                    def head(n):
                        hd.block(n)
                        hd.wait(kk_ready, 1)
                        hd(nc.gpsimd.tensor_tensor(rn[:, :, :], kk[:, :, :], kk[:, :, :], ALU.mult), kk2_ready)
                        hd.wait(G_ready, 1)
                        hd(nc.gpsimd.tensor_tensor(egx[:, :, :], G[:, :, :], sig[:, 0], ALU.subtract), gprev_ready)
                        hd.wait(k2_ready, 1)
                        hd.wait(exps_ready, 1)
                        for e in range(2):
                            h = half(e)
                            hd(nc.gpsimd.tensor_tensor(BK[h, :, :, 1 - e], chunks(k2[h]), chunks(egi[h]), ALU.mult),
                               kt_ready if e else head_pool)
                        hd.end("pool head")

                    def run(n, first, ahead):
                        s.block(n)
                        s.wait(mix_ready, 4)
                        s(copy(prev[:, :, 0:1], prev[:, :, T2:T2 + 1], ones[:, 0:MIX].unsqueeze(2)), carry_ready)
                        for j in range(NC):
                            for e in range(2):
                                s.wait(sm_ready, 2 * j + e + 1)
                                s(nc.gpsimd.tensor_tensor(ET[j][half(e), :, half(e)], SM[j][e][half(e), :, 0],
                                                          off16[half(e), :].unsqueeze(1).broadcast_to([HD, NP, HD]), ALU.mult),
                                  et_ready if e else pool_own)
                            for e in range(2):
                                o = half(1 - e)
                                s(copy(LA[e][o, :, j, 0], SM[j][e][o, :, 0], ones_of(o)), la_ready if e else pool_own)
                        s.wait(v_ready, 1)
                        for t, ready in ((SV, sv_ready), (UV, uv_ready)):
                            for e in range(2):
                                o = half(1 - e)
                                s(copy(t[e][o], Vt[o, 0], ones_of(o)), ready)
                        s.end("pool")
                        if ahead:
                            head(n + 1)

                    k = 0
                    for t in [*LA, *DT, *ET, *Qx, *SV]:
                        k += 1
                        nc.gpsimd.memset(t[:], 0.0).then_inc(zero_link, 1)
                        pool.wait_ge(zero_link, k)
                    nc.gpsimd.memset(prev[:, :, 0:1], 0.0).then_inc(zero_ready, 1)
                    pool.wait_ge(zero_ready, 1)
                    head(0)
                    each_block(pool, run)

                @block.vector
                def _(dve):
                    s = Steps(dve, dve_own)
                    hd = Steps(dve, head_dve)
                    nx = Steps(dve, None)
                    pv = Steps(dve, tail_dve)
                    fn = Steps(dve, None)

                    def shift(n, i):
                        nx.block(n)
                        t0, w, _ = GROUPS[MIX_GROUP[i]]
                        nx.count[mix_ready] = i
                        nx.wait(mix_in, MIXED[i])
                        nx(nc.vector.tensor_tensor(mix[:, t0:t0 + w, :], mix[:, t0:t0 + w, :], prev[:, t0:t0 + w, 0:T2], ALU.add), mix_ready)

                    def tanh():
                        hd.wait(eth_ready, 1)
                        hd(nc.vector.tensor_scalar_add(th[0:LORA, :], th[0:LORA, :], 1.0))
                        hd(nc.vector.reciprocal(th[0:LORA, :], th[0:LORA, :]))
                        hd(nc.vector.tensor_scalar(th[0:LORA, :], th[0:LORA, :], 2.0, -1.0, ALU.mult, ALU.add), th_ready)

                    def key():
                        hd(nc.vector.tensor_tensor(kk[:, :, :], mix[:, 4:8, :], wide(v("k_k", 0, NP)), ALU.mult), kk_ready)

                    def clamp(i):
                        hd.wait(e_ready, NP * (i + 1))
                        hd(nc.vector.tensor_scalar(sig[:, i], sig[:, i], LN_MAX, None, ALU.min), clamp_ready)

                    def decay_sum():
                        hd.wait(sig_ready, 1)
                        hd(nc.vector.tensor_tensor_scan(G[:, :, :].rearrange(flat), restart[:, :], sig[:, 0].rearrange(flat), 0.0,
                                                        ALU.mult, ALU.add), G_ready)

                    def new_key():
                        hd.wait(sig_ready, 2)
                        for p in range(NP):
                            hd(nc.vector.tensor_scalar(t2[:, p], sig[:, 1, p], v("k_a", p), oka[:, p:p + 1], ALU.mult, ALU.add), hold=(p == NP - 1))
                        hd(nc.vector.tensor_tensor(k2[:, :, :], mix[:, 4:8, :], t2[:, :, :], ALU.mult), k2_ready)
                        hd(nc.vector.tensor_tensor(rk[:, :, :], mix[:, 0:4, :], k2[:, :, :], ALU.mult), rk_ready)

                    def replaced_key():
                        hd.wait(rn_ready, 1)
                        hd(nc.vector.tensor_tensor(kk[:, :, :], kk[:, :, :], rn[:, :, :], ALU.mult))
                        hd(nc.vector.scalar_tensor_tensor(out=t2[:, :, :], in0=kk[:, :, :], scalar=-1.0, in1=sig[:, 1],
                                                          op0=ALU.mult, op1=ALU.mult))
                        hd.wait(exps_ready, 1)
                        for e in range(2):
                            h = half(e)
                            hd(nc.vector.tensor_tensor(BK[h, :, :, e], chunks(t2[h]), chunks(egi[h]), ALU.mult), hold=False)

                    def group_norm():
                        pv.wait(rs_ready, 1)
                        pv(nc.vector.tensor_tensor(Y[:, :, :], Y[:, :, :], rs[:, :, :], ALU.mult))
                        for p in range(NP):
                            pv(nc.vector.tensor_scalar(Y[:, p], Y[:, p], v("lnx_w", p), v("lnx_b", p), ALU.mult, ALU.add), hold=(p == NP - 1))
                        pv(nc.vector.tensor_tensor(Y[:, :, :], Y[:, :, :], bonus[:, :, :], ALU.add))
                        pv(nc.vector.tensor_tensor(Y[:, :, :], Y[:, :, :], rgate[:, :, :], ALU.mult), y2_ready)

                    def residual(n, h):
                        fn.block(n)
                        fn.count[h_ready] = h
                        if h == 0:
                            dve.wait_ge(h_loaded, n * 16 + 16)
                        fn.wait(out_ps, h + 1)
                        fn(nc.vector.tensor_tensor(hr[:, h * 512:(h + 1) * 512], bank[(4, 7)[h]][:, :], hr[:, h * 512:(h + 1) * 512], ALU.add), h_ready)

                    def final_norm(n):
                        fn.block(n)
                        fn.wait(hn_ready, 1)
                        fn(nc.vector.scalar_tensor_tensor(out=hr[:, :], in0=hr[:, :], scalar=hstat[:, 2:3], in1=fgain[:, :],
                                                          op0=ALU.mult, op1=ALU.mult), out_ready)

                    def per_head(t):
                        return t.rearrange("p (a b) -> p a b", b=HD)

                    def take_r(j):
                        s.wait(r_ps, j + 1)
                        s(nc.vector.tensor_copy(R[:, :, :].rearrange(flat), bank[5][:, 0:256]), r_ready)

                    def new_state(j):
                        s.wait(y_ps, j + 1)
                        for e in range(2):
                            h = half(e)
                            s(nc.vector.tensor_tensor(stmp[h], per_head(bank[7][h, 0:256]), SV[e][h], ALU.add), hold=bool(e))
                        for e in range(2):
                            h = half(e)
                            s(nc.vector.tensor_tensor(SV[e][h], stmp[h], dend[h, :, j:j + 1].broadcast_to([HD, NP, HD]), ALU.mult),
                              s_ready if e else None, hold=bool(e))

                    def run(n, first, ahead):
                        s.block(n)
                        hd.block(n + 1)
                        if not first:
                            pv.block(n - 1)
                        s.wait(exps_ready, 2)
                        for e in range(2):
                            h = half(e)
                            s(nc.vector.tensor_tensor(LA[e][h, :, :, 1], chunks(mix[h, 0:4]), chunks(sig[h, 0]), ALU.mult), hold=False)
                        s.wait(exps_ready, 3)
                        for e in range(2):
                            h = half(e)
                            s(nc.vector.tensor_tensor(LA[e][h, :, :, 0], chunks(kk[h]), chunks(egx[h]), ALU.mult), lhs_ready if e else None,
                              hold=False)
                        s(nc.vector.tensor_copy(dend[:, :, :].unsqueeze(3), chunks(sig[:, 0])[:, :, :, C - 1:C]), hold=False)
                        for j in range(NC):
                            for e in range(2):
                                s.wait(gram_ps, 2 * j + e + 1)
                                s(nc.vector.tensor_tensor(SM[j][e].rearrange("p a b c -> p a (b c)"),
                                                          bank[((2, 3), (4, 7))[j][e]][:, :].rearrange("p (a b) -> p a b", b=P),
                                                          gram_mask[:, :].unsqueeze(1).broadcast_to([P, NP, P]), ALU.mult), sm_ready)
                            for e in range(2):
                                h = half(e)
                                s(nc.vector.tensor_tensor(DT[j][h, :, h], SM[j][e][h, :, 0],
                                                          diag16[h, :].unsqueeze(1).broadcast_to([HD, NP, HD]), ALU.mult),
                                  dt_ready if e else None, hold=bool(e))
                            if j == 0 and not first:
                                shift(n, 3)
                        for j in range(NC):
                            for e in range(2):
                                h = half(e)
                                s(nc.vector.tensor_tensor(Q1[j][h], DT[j][h, :, h],
                                                          ident64[h, :].unsqueeze(1).broadcast_to([HD, NP, HD]), ALU.add),
                                  q1_ready if e else None, hold=bool(e))
                        if not first:
                            group_norm()
                        s.wait(bonus_ps, 1)
                        s(nc.vector.tensor_tensor(bonus[:, :, :].rearrange(flat), bank[1][:, :], mix[:, 8:12, :].rearrange(flat), ALU.mult),
                          prep_ready)
                        for i in range(6):
                            for j in range(NC):
                                s.wait(inv_ps, NC * (2 + i) + j + 1)
                                s(nc.vector.tensor_tensor(Qr[j][:, :, :].rearrange(flat), bank[2 + j][:, (i % 2) * 256:(i % 2) * 256 + 256],
                                                          Q1[j][:, :, :].rearrange(flat), ALU.add), horner_ready, hold=False)
                            if i == 0 and ahead:
                                shift(n + 1, 0)
                            if i == 1 and ahead:
                                tanh()
                            if i == 2:
                                s.wait(erg_ready, 1)
                                s(nc.vector.tensor_scalar(rgate[:, :, :], rgate[:, :, :], LN_MAX, None, ALU.min), gclamp_ready)
                                if not first:
                                    residual(n - 1, 0)
                            if i == 3 and ahead:
                                shift(n + 1, 1)
                            if i == 4 and not first:
                                residual(n - 1, 1)
                            if i == 5:
                                s.wait(gsig_ready, 1)
                                s(nc.vector.tensor_tensor(rgate[:, :, :], rgate[:, :, :], rg[:, :, :], ALU.mult), rgate_ready)
                        for j in range(NC):
                            s.wait(inv_ps, NC * 8 + j + 1)
                            s(nc.vector.tensor_tensor(QD[j][:, :, :].rearrange(flat), bank[2 + j][:, 0:256],
                                                      Q1[j][:, :, :].rearrange(flat), ALU.add))
                            for e in range(2):
                                s(nc.vector.tensor_copy(Qx[j][half(e), :, half(e)], QD[j][half(e)]), qd_ready if e else None, hold=bool(e))
                        for i in range(2):
                            for j in range(NC):
                                s.wait(inv_ps, NC * (11 + i) + j + 1)
                                s(nc.vector.tensor_tensor(Qr[j][:, :, :].rearrange(flat), bank[2 + j][:, i * 256:i * 256 + 256],
                                                          QD[j][:, :, :].rearrange(flat), ALU.add), g_ready, hold=False)
                            if i == 0 and not first:
                                final_norm(n - 1)
                        for j in range(NC):
                            s.wait(inv_ps, NC * 13 + j + 1)
                            for e in range(2):
                                h = half(e)
                                s(nc.vector.tensor_tensor(Qx[j][h, :, h], per_head(bank[2 + j][h, 0:256]), QD[j][h], ALU.add),
                                  q_ready if e else None, hold=bool(e))
                        take_r(0)
                        if ahead:
                            shift(n + 1, 2)
                            key()
                            clamp(0)
                        new_state(0)
                        if ahead:
                            clamp(1)
                            decay_sum()
                        take_r(1)
                        if ahead:
                            new_key()
                        new_state(1)
                        if ahead:
                            replaced_key()
                            hd.end("dve head")
                        s.end("dve")

                    dve.wait_ge(w2_loaded, 16 * (KT + 1))
                    for t in range(NP):
                        nc.vector.tensor_tensor(wo2[:, t, :], wo2[:, t, :], gate_row[:, :], ALU.mult).then_inc(set_link, 1)
                    dve.wait_ge(set_link, NP)
                    dve.sem_inc(wo2_ready, 1)
                    dve.wait_ge(zero_ready, 1)
                    hd.block(0)
                    shift(0, 0)
                    tanh()
                    for i in range(1, 4):
                        shift(0, i)
                    key()
                    clamp(0)
                    clamp(1)
                    decay_sum()
                    new_key()
                    replaced_key()
                    each_block(dve, run)
                    pv.block(N2 - 1)
                    group_norm()
                    residual(N2 - 1, 0)
                    residual(N2 - 1, 1)
                    final_norm(N2 - 1)

_INS = ["x", "c", "w_ada", "b_ada", "norm_gain", "w_in", "pool_w", "pool_scale", "mu", "w0", "w_lora_up", "a0",
        "a_lora_up", "k_k", "k_a", "r_k", "lnx_w", "lnx_b", "w_out", "final_gain"]


def kernel(**inputs):
    import numpy as np
    import concourse.bacc as bacc
    from concourse import mybir as _mybir
    from concourse.bass_utils import run_bass_kernel_spmd

    nc = bacc.Bacc("TRN2", target_bir_lowering=False, num_devices=1)
    arrays, args = {}, {}
    for name in _INS:
        a = np.ascontiguousarray(inputs[name])
        arrays[f"in_{name}"] = a
        args[name] = nc.dram_tensor(f"in_{name}", a.shape, _mybir.dt.from_np(a.dtype), kind="ExternalInput").ap()
    out = nc.dram_tensor("out_0", (1, SEQ, D), F32, kind="ExternalOutput").ap()
    build(nc, args, out)
    r = run_bass_kernel_spmd(nc, [arrays], core_ids=[0])
    return r.results[0]["out_0"]
```
